# Optimizing a Trainium2 kernel written in Bass

```python
import math
import jax, jax.numpy as jnp
from jax import lax
import numpy as np

D_MODEL = 2048
BATCH = 1
SEQ = 256
DEPTH = 1

CHUNK = 64
EPS = 1e-6
RW_HEADS = 16
RW_HEAD_DIM = 64
RW_WIDTH = RW_HEADS * RW_HEAD_DIM
RW_DECAY_RANK = 64
RW_ICL_RANK = 64
RW_GATE_RANK = 160
RW_GN_EPS = 64e-5
RW_SPLITS = (RW_WIDTH, RW_WIDTH, RW_WIDTH, RW_DECAY_RANK, RW_ICL_RANK, RW_GATE_RANK)
RW_IN = 3 * RW_WIDTH + RW_DECAY_RANK + RW_ICL_RANK + RW_GATE_RANK
SA_HEADS = 16
SA_HEAD_DIM = 64
SA_WIDTH = SA_HEADS * SA_HEAD_DIM
SA_SCALE = SA_HEAD_DIM ** -0.5
KV_RANK = 256
IDX_HEADS = 8
IDX_DIM = 64
IDX_SCALE = (IDX_HEADS * IDX_DIM) ** -0.5
TOPK_MAX = 256
Q_BLOCK = 128
REL_BUCKETS = 32
REL_MAX_DIST = 1024
N_BRANCHES = 2
IN_SPLITS = (RW_IN, SA_WIDTH, KV_RANK, IDX_HEADS * IDX_DIM, IDX_DIM, IDX_HEADS, N_BRANCHES * D_MODEL)
IN_TOTAL = RW_IN + SA_WIDTH + KV_RANK + IDX_HEADS * IDX_DIM + IDX_DIM + IDX_HEADS + N_BRANCHES * D_MODEL
PEER_HEADS = 8
PEER_KEYS = 128
PEER_EXPERTS = PEER_KEYS * PEER_KEYS
PEER_QDIM = 256
PEER_HALF = PEER_QDIM // 2
PEER_TOPK = 16
PEER_BLOCK = 128


def _split(x, sizes):
    idx = []
    acc = 0
    for s in sizes[:-1]:
        acc += s
        idx.append(acc)
    return jnp.split(x, idx, axis=-1)

def _rmsnorm(x, g):
    x32 = x.astype(jnp.float32)
    y = x32 * lax.rsqrt(jnp.mean(x32 * x32, axis=-1, keepdims=True) + EPS)
    return (y * g.astype(jnp.float32)).astype(x.dtype)

def _rel_bucket(rel):
    nb = REL_BUCKETS // 2
    max_exact = nb // 2
    ret = (rel > 0).astype(jnp.int32) * nb
    n = jnp.abs(rel)
    large = max_exact + (jnp.log(jnp.maximum(n, 1).astype(jnp.float32) / max_exact)
                         / math.log(REL_MAX_DIST / max_exact) * (nb - max_exact)).astype(jnp.int32)
    large = jnp.minimum(large, nb - 1)
    return ret + jnp.where(n < max_exact, n, large)

def _rwkv7_time_mix(p, shift_mix, w0, w_decay_up, a0, w_icl_up, w_gate_up, k_k, k_a, r_k, ln_x_w, ln_x_b):
    B, T, _ = p.shape
    H, N = RW_HEADS, RW_HEAD_DIM
    f32 = jnp.float32
    prev = jnp.pad(p, ((0, 0), (1, 0), (0, 0)))[:, :T]
    z = p + (prev - p) * shift_mix
    r, k, v, zw, za, zg = _split(z, RW_SPLITS)
    w_log = -jax.nn.softplus(-(w0 + jnp.tanh(zw) @ w_decay_up).astype(f32)) - 0.5
    decay = jnp.exp(-jnp.exp(w_log))
    a = jax.nn.sigmoid((a0 + za @ w_icl_up).astype(f32))
    g = jax.nn.sigmoid(zg) @ w_gate_up
    kf = k.astype(f32)
    kk = (kf * k_k.astype(f32)).reshape(B, T, H, N)
    kk = kk / jnp.maximum(jnp.linalg.norm(kk, axis=-1, keepdims=True), 1e-12)
    k4 = (kf * (1.0 + (a - 1.0) * k_a.astype(f32))).reshape(B, T, H, N)
    r4 = r.astype(f32).reshape(B, T, H, N)
    v4 = v.astype(f32).reshape(B, T, H, N)
    a4 = a.reshape(B, T, H, N)
    w4 = decay.reshape(B, T, H, N)

    def step(S, inp):
        r_t, k_t, v_t, kk_t, a_t, w_t = inp
        sa = jnp.einsum('bhvk,bhk->bhv', S, -kk_t)
        S = (S * w_t[:, :, None, :] + sa[..., None] * (kk_t * a_t)[:, :, None, :]
             + v_t[..., None] * k_t[:, :, None, :])
        return S, jnp.einsum('bhvk,bhk->bhv', S, r_t)

    xs = tuple(jnp.moveaxis(t, 1, 0) for t in (r4, k4, v4, kk, a4, w4))
    _, ys = lax.scan(step, jnp.zeros((B, H, N, N), f32), xs)
    y = jnp.moveaxis(ys, 0, 1)
    mean = jnp.mean(y, axis=-1, keepdims=True)
    var = jnp.mean(jnp.square(y - mean), axis=-1, keepdims=True)
    y = ((y - mean) * lax.rsqrt(var + RW_GN_EPS)).reshape(B, T, RW_WIDTH)
    y = y * ln_x_w.astype(f32) + ln_x_b.astype(f32)
    bonus = jnp.sum(r4 * k4 * r_k.astype(f32), axis=-1, keepdims=True) * v4
    y = (y + bonus.reshape(B, T, RW_WIDTH)) * g.astype(f32)
    return y.astype(p.dtype)

def _dsa_attention(q, c_kv, iq, ik, iw, kv_norm_g, w_uk, w_uv, rel_bias):
    B, T, _ = q.shape
    topk = min(TOPK_MAX, T // 4)
    f32 = jnp.float32
    c = _rmsnorm(c_kv, kv_norm_g)
    q_lat = jnp.einsum('bthd,hrd->bthr', q.reshape(B, T, SA_HEADS, SA_HEAD_DIM), w_uk)
    iq = iq.reshape(B, T, IDX_HEADS, IDX_DIM)
    iw = iw * IDX_SCALE
    key_chunk = jnp.arange(T) // CHUNK

    def block(i):
        s0 = i * Q_BLOCK
        qi = lax.dynamic_slice_in_dim(iq, s0, Q_BLOCK, axis=1)
        wi = lax.dynamic_slice_in_dim(iw, s0, Q_BLOCK, axis=1)
        ql = lax.dynamic_slice_in_dim(q_lat, s0, Q_BLOCK, axis=1)
        tq = s0 + jnp.arange(Q_BLOCK)
        score = jnp.einsum('bqhs,bqh->bqs', jax.nn.relu(jnp.einsum('bqhd,bsd->bqhs', qi, ik)), wi).astype(f32)
        allowed = key_chunk[None, :] <= (tq // CHUNK)[:, None]
        score = jnp.where(allowed[None], score, -jnp.inf)
        top_s, idx = lax.top_k(score, topk)
        valid = jnp.isfinite(top_s)
        c_sel = jax.vmap(lambda cb, ib: cb[ib])(c, idx)
        logits = jnp.einsum('bqhr,bqkr->bqhk', ql, c_sel).astype(f32) * SA_SCALE
        bias = rel_bias[_rel_bucket(idx - tq[None, :, None])]
        logits = logits + jnp.transpose(bias, (0, 1, 3, 2)).astype(f32)
        logits = jnp.where(valid[:, :, None, :], logits, -jnp.inf)
        pr = jax.nn.softmax(logits, axis=-1).astype(c.dtype)
        o_lat = jnp.einsum('bqhk,bqkr->bqhr', pr, c_sel)
        o = jnp.einsum('bqhr,hrd->bqhd', o_lat, w_uv)
        return o.reshape(B, Q_BLOCK, SA_WIDTH)

    out = lax.map(block, jnp.arange(T // Q_BLOCK))
    return jnp.moveaxis(out, 0, 1).reshape(B, T, SA_WIDTH)

def _peer_ffn(h, w_query, sub_keys, expert_u, expert_v):
    B, T, D = h.shape
    q = (h @ w_query).reshape(B, T, PEER_HEADS, 2, PEER_HALF)
    s = jnp.einsum('bthcq,hcnq->bthcn', q, sub_keys).astype(jnp.float32)
    s1, i1 = lax.top_k(s[..., 0, :], PEER_TOPK)
    s2, i2 = lax.top_k(s[..., 1, :], PEER_TOPK)
    cand = (s1[..., :, None] + s2[..., None, :]).reshape(B, T, PEER_HEADS, PEER_TOPK * PEER_TOPK)
    cand_id = (i1[..., :, None] * PEER_KEYS + i2[..., None, :]).reshape(B, T, PEER_HEADS, PEER_TOPK * PEER_TOPK)
    top_s, pos = lax.top_k(cand, PEER_TOPK)
    eid = jnp.take_along_axis(cand_id, pos, axis=-1)
    gate = jax.nn.softmax(top_s, axis=-1).astype(h.dtype)
    nb = (B * T) // PEER_BLOCK
    hb = h.reshape(nb, PEER_BLOCK, D)
    eb = eid.reshape(nb, PEER_BLOCK, PEER_HEADS, PEER_TOPK)
    gb = gate.reshape(nb, PEER_BLOCK, PEER_HEADS, PEER_TOPK)

    def blk(args):
        hx, e, gt = args
        act = jax.nn.gelu(jnp.einsum('nd,nhkd->nhk', hx, expert_u[e]), approximate=False)
        return jnp.einsum('nhk,nhkd->nd', gt * act, expert_v[e])

    return lax.map(blk, (hb, eb, gb)).reshape(B, T, D)

def first_inputs(seed: int = 0) -> dict:
    key = jax.random.key(seed)
    ks = iter(jax.random.split(key, 40))
    L, D = DEPTH, D_MODEL
    nrm = lambda shape, scale: jax.random.normal(next(ks), shape, jnp.float32) * scale
    uni = lambda shape, lo, hi: jax.random.uniform(next(ks), shape, jnp.float32, lo, hi)
    gain = lambda shape: 1.0 + nrm(shape, 0.02)
    return {
        'x': nrm((BATCH, SEQ, D), 1.0),
        'norm_mix_g': gain((L, D)),
        'w_in': nrm((L, D, IN_TOTAL), D ** -0.5),
        'shift_mix': uni((L, RW_IN), 0.0, 1.0),
        'w0': uni((L, RW_WIDTH), -4.0, 0.0),
        'w_decay_up': nrm((L, RW_DECAY_RANK, RW_WIDTH), 0.3 * RW_DECAY_RANK ** -0.5),
        'a0': nrm((L, RW_WIDTH), 0.3),
        'w_icl_up': nrm((L, RW_ICL_RANK, RW_WIDTH), RW_ICL_RANK ** -0.5),
        'w_gate_up': nrm((L, RW_GATE_RANK, RW_WIDTH), RW_GATE_RANK ** -0.5),
        'k_k': 0.85 + nrm((L, RW_WIDTH), 0.05),
        'k_a': 1.0 + nrm((L, RW_WIDTH), 0.05),
        'r_k': nrm((L, RW_HEADS, RW_HEAD_DIM), 0.1),
        'ln_x_w': gain((L, RW_WIDTH)),
        'ln_x_b': nrm((L, RW_WIDTH), 0.02),
        'kv_norm_g': gain((L, KV_RANK)),
        'w_uk': nrm((L, SA_HEADS, KV_RANK, SA_HEAD_DIM), KV_RANK ** -0.5),
        'w_uv': nrm((L, SA_HEADS, KV_RANK, SA_HEAD_DIM), KV_RANK ** -0.5),
        'rel_bias': nrm((REL_BUCKETS, SA_HEADS), 0.5),
        'w_branch_rwkv': nrm((L, RW_WIDTH, D), RW_WIDTH ** -0.5),
        'w_branch_dsa': nrm((L, SA_WIDTH, D), SA_WIDTH ** -0.5),
        'w_out': nrm((L, D, D), D ** -0.5),
        'norm_ffn_g': gain((L, D)),
        'w_peer_query': nrm((L, D, PEER_HEADS * PEER_QDIM), D ** -0.5),
        'peer_sub_keys': nrm((L, PEER_HEADS, 2, PEER_KEYS, PEER_HALF), PEER_HALF ** -0.5),
        'peer_u': nrm((L, PEER_EXPERTS, D), D ** -0.5),
        'peer_v': nrm((L, PEER_EXPERTS, D), 0.25),
        'norm_final_g': gain((D,)),
    }

def first_block(x, norm_mix_g, w_in, shift_mix, w0, w_decay_up, a0, w_icl_up, w_gate_up, k_k, k_a, r_k,
              ln_x_w, ln_x_b, kv_norm_g, w_uk, w_uv, rel_bias, w_branch_rwkv, w_branch_dsa, w_out,
              norm_ffn_g, w_peer_query, peer_sub_keys, peer_u, peer_v, norm_final_g):
    h = x
    for l in range(DEPTH):
        xn = _rmsnorm(h, norm_mix_g[l])
        p_rw, q, c_kv, iq, ik, iw, gates = _split(xn @ w_in[l], IN_SPLITS)
        y_a = _rwkv7_time_mix(p_rw, shift_mix[l], w0[l], w_decay_up[l], a0[l], w_icl_up[l], w_gate_up[l],
                              k_k[l], k_a[l], r_k[l], ln_x_w[l], ln_x_b[l]) @ w_branch_rwkv[l]
        y_b = _dsa_attention(q, c_kv, iq, ik, iw, kv_norm_g[l], w_uk[l], w_uv[l], rel_bias) @ w_branch_dsa[l]
        g_a, g_b = jnp.split(jax.nn.sigmoid(gates), N_BRANCHES, axis=-1)
        h = h + (g_a * y_a + g_b * y_b) @ w_out[l]
        h = h + _peer_ffn(_rmsnorm(h, norm_ffn_g[l]), w_peer_query[l], peer_sub_keys[l], peer_u[l], peer_v[l])
    return _rmsnorm(h, norm_final_g)


DEPTH_2 = 2

N_A_LAYERS = DEPTH_2 // 2
N_B_LAYERS = DEPTH_2 - N_A_LAYERS
HG_KDIM = 128
HG_HEADS = D_MODEL // HG_KDIM
HG_VDIM = D_MODEL // HG_HEADS
HG_FDIM = HG_HEADS * HG_KDIM
HG_BLOCK = CHUNK // 4
FOX_HDIM = 128
FOX_HEADS = D_MODEL // FOX_HDIM
FORGET_BIAS_INIT = 2.0


def rmsnorm(x, w):
    xf = x.astype(jnp.float32)
    y = xf * lax.rsqrt(jnp.mean(xf * xf, axis=-1, keepdims=True) + EPS)
    return (y * w.astype(jnp.float32)).astype(x.dtype)

def head_rmsnorm(x, w):
    xf = x.astype(jnp.float32)
    return xf * lax.rsqrt(jnp.mean(xf * xf, axis=-1, keepdims=True) + EPS) * w.astype(jnp.float32)

def hgrn2_chunkwise(q, k, v, g):
    B, H, T, dk = q.shape
    dv = v.shape[-1]
    n = T // HG_BLOCK

    def to_blocks(a):
        return jnp.moveaxis(a.reshape(B, H, n, HG_BLOCK, a.shape[-1]), 2, 0)

    mask = jnp.tril(jnp.ones((HG_BLOCK, HG_BLOCK), dtype=bool))[:, :, None]

    def step(S, blk):
        qc, kc, vc, gc = blk
        b = jnp.cumsum(gc, axis=-2)
        diff = b[..., :, None, :] - b[..., None, :, :]
        decay = jnp.exp(jnp.where(mask, diff, -jnp.inf))
        A = jnp.einsum('bhtd,bhsd,bhtsd->bhts', qc, kc, decay)
        o = (jnp.einsum('bhts,bhse->bhte', A, vc)
             + jnp.einsum('bhtd,bhde->bhte', qc * jnp.exp(b), S))
        b_last = b[..., -1:, :]
        S = (jnp.exp(b_last[..., 0, :])[..., None] * S
             + jnp.einsum('bhsd,bhse->bhde', kc * jnp.exp(b_last - b), vc))
        return S, o

    S0 = jnp.zeros((B, H, dk, dv), jnp.float32)
    _, o = lax.scan(step, S0, (to_blocks(q), to_blocks(k), to_blocks(v), to_blocks(g)))
    return jnp.moveaxis(o, 0, 2).reshape(B, H, T, dv)

def hgrn2_layer(x, norm_w, w_in, lb, out_norm_w, w_out):
    B, T, _ = x.shape
    h = rmsnorm(x, norm_w)
    proj = h @ w_in
    q = proj[..., :HG_FDIM]
    fz = proj[..., HG_FDIM:2 * HG_FDIM]
    i = proj[..., 2 * HG_FDIM:2 * HG_FDIM + D_MODEL]
    gate = proj[..., 2 * HG_FDIM + D_MODEL:]
    heads_k = lambda a: a.reshape(B, T, HG_HEADS, HG_KDIM).astype(jnp.float32).transpose(0, 2, 1, 3)
    q, fz = heads_k(q), heads_k(fz)
    i = i.reshape(B, T, HG_HEADS, HG_VDIM).astype(jnp.float32).transpose(0, 2, 1, 3)
    lb = lb.reshape(HG_HEADS, 1, HG_KDIM)
    log_f = jnp.logaddexp(jnp.log(lb), jnp.log1p(-lb) + jax.nn.log_sigmoid(fz))
    k = (1.0 - lb) * jax.nn.sigmoid(-fz)
    o = hgrn2_chunkwise(q, k, i, log_f)
    o = head_rmsnorm(o.transpose(0, 2, 1, 3), out_norm_w.reshape(HG_HEADS, HG_VDIM))
    o = o.reshape(B, T, D_MODEL) * jax.nn.silu(gate.astype(jnp.float32))
    return x + (o.astype(x.dtype) @ w_out)

def shared_kv(x, norm_w, w_kvf, f_bias, k_norm_w):
    B, T, _ = x.shape
    h = rmsnorm(x, norm_w)
    kvf = h @ w_kvf
    k = kvf[..., :D_MODEL].reshape(B, T, FOX_HEADS, FOX_HDIM)
    v = kvf[..., D_MODEL:2 * D_MODEL].reshape(B, T, FOX_HEADS, FOX_HDIM)
    fz = kvf[..., 2 * D_MODEL:].astype(jnp.float32) + f_bias.astype(jnp.float32)
    k = head_rmsnorm(k, k_norm_w).transpose(0, 2, 1, 3)
    v = v.astype(jnp.float32).transpose(0, 2, 1, 3)
    F = jnp.cumsum(jax.nn.log_sigmoid(fz), axis=1).transpose(0, 2, 1)
    return k, v, F

def forgetting_attention(q, k, v, F):
    T = q.shape[2]
    scale = FOX_HDIM ** -0.5
    local = jnp.arange(Q_BLOCK)
    outs = []
    for blk in range(T // Q_BLOCK):
        q0 = blk * Q_BLOCK
        kend = q0 + Q_BLOCK
        s = (jnp.einsum('bhqd,bhkd->bhqk', q[:, :, q0:kend], k[:, :, :kend]) * scale
             + F[:, :, q0:kend, None] - F[:, :, None, :kend])
        causal = (q0 + local)[:, None] >= jnp.arange(kend)[None, :]
        p = jax.nn.softmax(jnp.where(causal, s, -jnp.inf), axis=-1)
        outs.append(jnp.einsum('bhqk,bhkd->bhqd', p, v[:, :, :kend]))
    return jnp.concatenate(outs, axis=2)

def fox_layer(x, norm_w, w_in, q_norm_w, out_norm_w, w_out, k, v, F):
    B, T, _ = x.shape
    h = rmsnorm(x, norm_w)
    proj = h @ w_in
    q = proj[..., :D_MODEL].reshape(B, T, FOX_HEADS, FOX_HDIM)
    gate = proj[..., D_MODEL:]
    q = head_rmsnorm(q, q_norm_w).transpose(0, 2, 1, 3)
    o = forgetting_attention(q, k, v, F)
    o = head_rmsnorm(o.transpose(0, 2, 1, 3), out_norm_w.reshape(FOX_HEADS, FOX_HDIM))
    o = o.reshape(B, T, D_MODEL) * jax.nn.silu(gate.astype(jnp.float32))
    return x + (o.astype(x.dtype) @ w_out)

def second_inputs(seed: int = 0) -> dict:
    key = jax.random.key(seed)
    ks = jax.random.split(key, 16)
    D = D_MODEL
    s = D ** -0.5
    nrm = jax.random.normal
    return {
        "x": nrm(ks[0], (BATCH, SEQ, D), jnp.float32),
        "a_norm_w": 1.0 + 0.02 * nrm(ks[1], (N_A_LAYERS, D), jnp.float32),
        "a_w_in": s * nrm(ks[2], (N_A_LAYERS, D, 2 * HG_FDIM + 2 * D), jnp.float32),
        "a_lb_logits": 0.1 * nrm(ks[3], (N_A_LAYERS, HG_FDIM), jnp.float32),
        "a_out_norm_w": 1.0 + 0.02 * nrm(ks[4], (N_A_LAYERS, D), jnp.float32),
        "a_w_out": s * nrm(ks[5], (N_A_LAYERS, D, D), jnp.float32),
        "kv_norm_w": 1.0 + 0.02 * nrm(ks[6], (D,), jnp.float32),
        "kv_w": s * nrm(ks[7], (D, 2 * D + FOX_HEADS), jnp.float32),
        "kv_f_bias": FORGET_BIAS_INIT + 0.1 * nrm(ks[8], (FOX_HEADS,), jnp.float32),
        "k_norm_w": 1.0 + 0.02 * nrm(ks[9], (FOX_HDIM,), jnp.float32),
        "b_norm_w": 1.0 + 0.02 * nrm(ks[10], (N_B_LAYERS, D), jnp.float32),
        "b_w_in": s * nrm(ks[11], (N_B_LAYERS, D, 2 * D), jnp.float32),
        "b_q_norm_w": 1.0 + 0.02 * nrm(ks[12], (N_B_LAYERS, FOX_HDIM), jnp.float32),
        "b_out_norm_w": 1.0 + 0.02 * nrm(ks[13], (N_B_LAYERS, D), jnp.float32),
        "b_w_out": s * nrm(ks[14], (N_B_LAYERS, D, D), jnp.float32),
    }

def second_block(x, a_norm_w, a_w_in, a_lb_logits, a_out_norm_w, a_w_out,
              kv_norm_w, kv_w, kv_f_bias, k_norm_w,
              b_norm_w, b_w_in, b_q_norm_w, b_out_norm_w, b_w_out):
    lb_all = jnp.cumsum(jax.nn.softmax(a_lb_logits.astype(jnp.float32), axis=0), axis=0)
    lb_all = lb_all - lb_all[0:1]
    k = v = F = None
    for layer in range(DEPTH_2):
        if layer < N_A_LAYERS:
            x = hgrn2_layer(x, a_norm_w[layer], a_w_in[layer], lb_all[layer],
                            a_out_norm_w[layer], a_w_out[layer])
        else:
            if layer == N_A_LAYERS:
                k, v, F = shared_kv(x, kv_norm_w, kv_w, kv_f_bias, k_norm_w)
            j = layer - N_A_LAYERS
            x = fox_layer(x, b_norm_w[j], b_w_in[j], b_q_norm_w[j], b_out_norm_w[j],
                          b_w_out[j], k, v, F)
    return x


def setup_inputs(seed=0):
    out = dict(first_inputs(seed))
    for name, value in second_inputs(seed + 1).items():
        if name != "x":
            out[name + "_2"] = value
    return out


def reference(
    x, norm_mix_g, w_in, shift_mix, w0, w_decay_up, a0, w_icl_up, w_gate_up, k_k, k_a, r_k,
    ln_x_w, ln_x_b, kv_norm_g, w_uk, w_uv, rel_bias, w_branch_rwkv, w_branch_dsa, w_out,
    norm_ffn_g, w_peer_query, peer_sub_keys, peer_u, peer_v, norm_final_g, a_norm_w_2, a_w_in_2,
    a_lb_logits_2, a_out_norm_w_2, a_w_out_2, kv_norm_w_2, kv_w_2, kv_f_bias_2, k_norm_w_2,
    b_norm_w_2, b_w_in_2, b_q_norm_w_2, b_out_norm_w_2, b_w_out_2,
):
    x = first_block(
        x, norm_mix_g, w_in, shift_mix, w0, w_decay_up, a0, w_icl_up, w_gate_up, k_k, k_a, r_k,
        ln_x_w, ln_x_b, kv_norm_g, w_uk, w_uv, rel_bias, w_branch_rwkv, w_branch_dsa, w_out,
        norm_ffn_g, w_peer_query, peer_sub_keys, peer_u, peer_v, norm_final_g,
    )
    return second_block(
        x, a_norm_w_2, a_w_in_2, a_lb_logits_2, a_out_norm_w_2, a_w_out_2, kv_norm_w_2, kv_w_2,
        kv_f_bias_2, k_norm_w_2, b_norm_w_2, b_w_in_2, b_q_norm_w_2, b_out_norm_w_2, b_w_out_2,
    )


_drawn_inputs = setup_inputs


def setup_inputs(seed=0):
    import zlib

    import numpy as np

    out = dict(_drawn_inputs(seed))
    spreads = {}
    factors = {'ln_x_w': 2.918,
     'kv_norm_g': 3.665,
     'a_out_norm_w_2': 4.53,
     'kv_norm_w_2': 4.888,
     'kv_f_bias_2': 2.699,
     'k_norm_w_2': 8.0,
     'b_norm_w_2': 4.749,
     'b_q_norm_w_2': 8.0,
     'b_out_norm_w_2': 6.084}
    for name, (base, spread) in spreads.items():
        noise = np.random.default_rng([zlib.crc32(name.encode()), seed]).standard_normal(out[name].shape)
        drawn = base * np.exp(spread * noise) if base else spread * noise
        out[name] = __import__('jax').numpy.asarray(drawn.astype(out[name].dtype))
    for name, factor in factors.items():
        out[name] = (out[name] * factor).astype(out[name].dtype)
    return out
```

```python
import math

import numpy as np

P = 128
T = 256
NT = T // P
D = 2048
KC = D // P
UNIT = 2048
SLOTS = 4
EPS = 1e-6
NEG = -1e30
TAKEN = -2e30

RW = 1024
RWH = 16
HD = 64
CH = 32
NCH = P // CH
RW_IN = 3 * RW + 64 + 64 + 160
GN_EPS = 64e-5
DECAY = math.exp(-0.5)
C_ZS = 3 * RW
C_Q = C_ZS + 512
C_IQ = C_Q + 1024
C_KV = C_IQ + 512
C_IW = C_KV + 256
C_IK = C_IW + 8
PW = C_KV + 512
SA_SCALE = 64 ** -0.5
IDX_SCALE = (8 * 64) ** -0.5
TOPK = 64
PK = 128
PH = 8
PT = 16
HH = 16
LEV = 7
FSCALE = 128 ** -0.5

STREAM = [("w_in", 19), ("br_a", 2), ("br_b", 2), ("w_out", 4), ("wq", 4), ("u0", 16), ("v0", 16), ("u1", 16), ("v1", 16),
          ("a_in", 16), ("a_out", 4), ("kv", 8), ("b_in", 8), ("b_out", 4)]
GROUP = {}
_g = 0
for _n, _k in STREAM:
    GROUP[_n] = _g
    _g += _k
GROUPS = _g


def rel_bucket(rel):
    nb, exact = 16, 8
    n = np.abs(rel)
    large = exact + (np.log(np.maximum(n, 1).astype(np.float32) / np.float32(exact))
                     / np.float32(math.log(1024 / exact)) * np.float32(nb - exact)).astype(np.int32)
    return (rel > 0) * nb + np.where(n < exact, n, np.minimum(large, nb - 1))


def constants():
    u, t = np.meshgrid(np.arange(P), np.arange(P), indexing="ij")
    same = u // CH == t // CH
    f = lambda m: m.astype(np.float32)
    c = {}
    c["ident"] = f(u == t)
    c["strict"] = f(same & (u < t))
    c["incl"] = f(same & (u <= t))
    c["suffix"] = f(same & (u > t))
    c["chunk"] = f(np.arange(P)[:, None] // CH == np.arange(NCH)[None])
    c["iota"] = f(t)
    c["anti"] = f(u + t == P - 1)
    c["tri"] = f(u <= t)
    c["ones"] = np.ones((P, P), np.float32)
    c["causal"] = np.where(t <= u, 0.0, NEG).astype(np.float32)
    p, j, tt = np.meshgrid(np.arange(P), np.arange(8), np.arange(CH), indexing="ij")
    c["unit_x"] = f(tt == 8 * (p // 32) + j).reshape(P, 256)
    tg = np.arange(P)[:, None, None] + P * np.arange(NT)[None, :, None]
    s = np.arange(T)[None, None]
    c["limit"] = np.where(s // 64 <= tg // 64, 3e38, NEG).astype(np.float32).reshape(P, NT * T)
    d = np.zeros((P, 512), np.float32)
    d[rel_bucket(np.arange(-255, 256)), np.arange(511)] = 1.0
    c["bucket"] = d
    dm, mk = [], []
    dm.append(f(u > t))
    for l in range(LEV):
        m = 1 << l
        mid = (t // (2 * m)) * 2 * m + m
        dm.append(np.where(t >= mid, f((u >= mid) & (u <= t)), f((u > t) & (u < mid))))
        mk.append(f((u // (2 * m) == t // (2 * m)) & (u % (2 * m) < m) & (t % (2 * m) >= m)))
    dm.append(f(u <= t))
    mk.append(f(u == t))
    c["dm"] = np.concatenate(dm, 1)
    c["levels"] = np.concatenate(mk, 1)
    sel = np.zeros((P, HH, P), np.float32)
    for h in range(HH):
        sel[h, h] = 1.0
    c["sel"] = sel.reshape(P, HH * P)
    return c


def build(nc, dram, consts):
    import concourse.bass as bass
    from concourse import mybir

    F32 = mybir.dt.float32
    F32R = mybir.dt.float32r
    U32 = mybir.dt.uint32
    ALU = mybir.AluOpType
    ACT = mybir.ActivationFunctionType
    X = mybir.AxisListType.X
    ds = bass.ds

    sems = {}

    def S(name):
        if name not in sems:
            sems[name] = nc.alloc_semaphore(name)
        return sems[name]

    def recycle():
        kept = ("landed", "hi", "lo", "norm_", "unit_used", "psum_free", "turn_hi", "turned", "x_back")
        old = [n for n in sems if not n.startswith(kept)]
        with nc.Block() as block:
            @block.sync
            def _(sp):
                for n in old:
                    sp.sem_clear(sems[n])
        for n in old:
            nc.release_semaphore(sems.pop(n))

    nc.alloc_sbuf_tensor("arena", (P, (nc.sbuf_usable_end - 16512 - 64) // 4), F32)
    top = nc.sbuf_usable_end
    bump = [16512]
    names = [0]

    def sb(name, shape, dt=F32):
        n = int(np.prod(shape[1:])) * 4
        h = nc.alloc_sbuf_tensor_at(name, tuple(shape), dt, offset=bump[0])
        bump[0] += (n + 31) // 32 * 32
        assert bump[0] <= top, (name, bump[0], top)
        return h

    def over(name, shape, dt, offset):
        return nc.alloc_sbuf_tensor_at(name, tuple(shape), dt, offset=offset)

    PS = nc.alloc_psum_tensor("PS", (P, 8, 512), F32)

    lo_w = [over(f"lo_w{i}", (P, UNIT), F32R, bump[0] + i * UNIT * 4) for i in range(SLOTS)]
    ring = [sb(f"ring{i}", (P, UNIT)) for i in range(SLOTS)]
    hi_base = (top - SLOTS * UNIT * 4) // 32 * 32
    hi_w = [over(f"hi_w{i}", (P, UNIT), F32R, hi_base + i * UNIT * 4) for i in range(SLOTS)]
    x = sb("x", (P, NT, D))
    lo_x = over("lo_x", (P, KC, T), F32R, bump[0])
    xT = sb("xT", (P, KC, T))
    hi_x = over("hi_x", (P, KC, T), F32R, bump[0])
    spare_at = bump[0]
    bump[0] += KC * T * 4
    ident = sb("ident", (P, P))
    incl3 = sb("incl3", (P, 3, P))
    chunk = sb("chunk", (P, NCH))
    gcol = sb("gcol", (P, KC))
    rstat = sb("rstat", (P, 8))
    base = bump[0]

    def scratch(name, shape):
        return nc.dram_tensor(name, shape, F32).ap()

    def bcast(name, n=None, off=0):
        a = dram[name]
        n = n or int(np.prod(a.shape))
        return bass.AP(a.tensor, off, [[0, P], [1, n]])

    def cload(eng, dst, name, sem, rows=P):
        return eng.dma_start(dst, consts[name][0:rows]).then_inc(sem, 16)

    wst = dram["wstream"]

    def stream(sp, name):
        g0, n = GROUP[name], dict(STREAM)[name]
        n = min(n, GROUPS - 1 - g0)
        if n <= 0:
            return
        with sp.Fori(g0, g0 + n) as g:
            for s in range(SLOTS):
                sp.wait_ge(S("unit_used"), g * SLOTS + s + 1)
                sp.dma_start(ring[s][:], wst[ds(g * SLOTS + SLOTS + s, 1)].rearrange("a p f -> p (a f)"))\
                    .then_inc(S(f"landed{s}"), 16)

    chunks = [0]

    def split_hi(a, g, s):
        a.wait_ge(S(f"landed{s}"), g * 16 + 16)
        a.copy(hi_w[s][:], ring[s][:]).then_inc(S(f"hi{s}"), 1)

    def split_lo(v, g, s):
        v.wait_ge(S(f"hi{s}"), g + 1)
        v.tensor_tensor(lo_w[s][:], ring[s][:], hi_w[s][:].bitcast(F32), ALU.subtract).then_inc(S(f"lo{s}"), 1)

    def dense(t, name, n, kc, a_T, at=0):
        g0 = GROUP[name] + (at if kc == 16 else at // 2)
        n0 = chunks[0]

        def one(j, c, free):
            if free:
                for tt in range(NT):
                    t.wait_ge(S(f"psum_free{tt}"), j * 2 + (n0 + c - 1))
            for q in range(kc // 4):
                slot = q if kc == 16 else 2 * c + q
                g = j * 2 + (g0 + c) if kc == 16 else j + g0
                t.wait_ge(S(f"lo{slot}"), g + 1)
                for tt in range(NT):
                    for k in range(4):
                        kk = q * 4 + k
                        for p, (xa, wa) in enumerate(((0, hi_w), (0, lo_w), (1, hi_w))):
                            mm = nc.tensor.matmul(PS[:, 2 * c + tt, :], a_T[xa][:, kk, tt * P:(tt + 1) * P],
                                                  wa[slot][:, k * 512:(k + 1) * 512],
                                                  start=(kk == 0 and p == 0), stop=(kk == kc - 1 and p == 2))
                mm.then_inc(S("unit_used"), 1)

        one(0, 0, False)
        if n > 1:
            one(0, 1, False)
        if n // 2 > 1:
            with t.Fori(1, n // 2) as j:
                one(j, 0, True)
                one(j, 1, True)
        if n > 1 and n % 2:
            one(n // 2, 0, True)

    def begin(eng, split, name, kc):
        for q in range(kc // 4):
            split(eng, GROUP[name], q)

    def evac(eng, split, name, n, kc, tiles, f, at=0, first=True, last=True,
             before=None, after=None, ending=None, free=True):
        per = kc // 4
        u0 = GROUP[name] * SLOTS + at * per
        g0 = u0 // SLOTS

        def ahead(j, c, q):
            if kc == 16:
                split(eng, j * 2 + (g0 + c + 1), q)
            else:
                split(eng, j + (g0 + c), q + (0 if c else per))

        def one(j, c, more=True):
            if before:
                before(j * 2 + c)
            if more:
                for q in range(per - 1):
                    ahead(j, c, q)
            if tiles:
                eng.wait_ge(S("unit_used"), j * (2 * per) + (u0 + per * (c + 1)))
            for tt in tiles:
                m = f(tt, PS[:, 2 * c + tt, :], j * 2 + c, c)
                if free:
                    m.then_inc(S(f"psum_free{tt}"), 1)
            if after:
                after(j, c)
            if more:
                ahead(j, c, per - 1)
            if ending:
                ending(j * 2 + c)

        if first:
            begin(eng, split, name, kc)
        pairs = n // 2
        looped = pairs - 1 if last and n % 2 == 0 else pairs
        if looped > 1:
            with eng.Fori(0, looped) as j:
                one(j, 0)
                one(j, 1)
        elif looped == 1:
            one(0, 0)
            one(0, 1)
        if looped < pairs:
            one(pairs - 1, 0)
            one(pairs - 1, 1, False)
        if n % 2:
            one(pairs, 0, not last)

    def to(dst, off=0):
        def f_for(eng, is_act):
            def f(tt, bank, c, par):
                o = dst[:, tt, ds(c * 512 + off, 512)]
                return eng.copy(o, bank) if is_act else eng.tensor_copy(o, bank)
            return f
        return f_for

    norms = [0, 0]
    turns = [0]

    def part(b):
        return slice((b % 4) * 4, (b % 4) * 4 + 4), slice((b // 4) * P, (b // 4 + 1) * P)

    def norm_T(gain, stats=True, xs=None):
        i = norms[0]
        at = bump[0]
        if xs is None:
            bump[0] = base
            xs = sb(f"xs{i}", (P, NT, D))
            junk = sb(f"junk{i}", (P, D))
        scaled, turned, loaded, sq = (S("norm_" + w) for w in ("scaled", "turned", "gain", "root"))
        k, ks = norms
        norms[0] += 1
        norms[1] += stats
        with nc.Block() as block:
            @block.scalar
            def _(a):
                a.dma_start(gcol[:], dram[gain]).then_inc(loaded, 16)
                if stats:
                    for tt in range(NT):
                        a.activation(junk[:], x[:, tt, :], ACT.Square, accum_out=rstat[:, tt:tt + 1])
                        a.drain()
                        a.activation(rstat[:, 2 + tt:3 + tt], rstat[:, tt:tt + 1], ACT.Sqrt,
                                     bias=EPS, scale=1.0 / D).then_inc(sq, 1)
                for b in range(8):
                    a.wait_ge(S("norm_out"), 8 * k + b + 1)
                    r, c = part(b)
                    a.copy(hi_x[:, r, c], xT[:, r, c]).then_inc(S("norm_hi"), 1)

            @block.vector
            def _(v):
                for tt in range(NT):
                    if stats:
                        v.wait_ge(sq, NT * ks + tt + 1)
                        v.reciprocal(rstat[:, 4 + tt:5 + tt], rstat[:, 2 + tt:3 + tt])
                        v.drain()
                    v.tensor_scalar(xs[:, tt, :], x[:, tt, :], rstat[:, 4 + tt:5 + tt], None, ALU.mult)\
                        .then_inc(scaled, 1)
                v.wait_ge(loaded, 16 * k + 16)
                for tt in range(NT):
                    for b in range(4):
                        v.wait_ge(turned, 8 * k + tt * 4 + b + 1)
                        v.tensor_tensor(xT[:, b * 4:b * 4 + 4, tt * P:(tt + 1) * P],
                                        PS[:, tt * 4 + b, :].rearrange("p (k c) -> p k c", k=4),
                                        gcol[:, b * 4:b * 4 + 4].unsqueeze(2).broadcast_to((P, 4, P)),
                                        ALU.mult).then_inc(S("norm_out"), 1)
                for b in range(8):
                    v.wait_ge(S("norm_hi"), 8 * k + b + 1)
                    r, c = part(b)
                    v.tensor_tensor(lo_x[:, r, c], xT[:, r, c], hi_x[:, r, c].bitcast(F32), ALU.subtract)

            @block.tensor
            def _(t):
                for tt in range(NT):
                    t.wait_ge(scaled, NT * k + tt + 1)
                    for b in range(4):
                        for q in range(4):
                            kk = b * 4 + q
                            mm = nc.tensor.transpose(PS[:, tt * 4 + b, q * P:(q + 1) * P],
                                                     xs[:, tt, kk * P:(kk + 1) * P], ident[:])
                        mm.then_inc(turned, 1)
        bump[0] = base if stats else at

    with nc.Block() as block:
        @block.sync
        def _(sp):
            sp.dma_start(x[:], dram["x"].rearrange("(t p) d -> p t d", p=P)).then_inc(S("x_in"), 16)
            cload(sp, ident[:], "ident", S("x_in"))
            for k, n in enumerate(("strict", "incl", "suffix")):
                cload(sp, incl3[:, k, :], n, S("x_in"))
            cload(sp, chunk[:], "chunk", S("x_in"))
            for s in range(SLOTS):
                sp.dma_start(ring[s][:], wst[s]).then_inc(S(f"landed{s}"), 16)
            sp.wait_ge(S("x_in"), 96)
    norm_T("norm_mix_g")
    X_ = (hi_x, lo_x)

    PR = sb("PR", (P, NT, PW))
    gstage = sb("gstage", (P, 2, NT, 512))
    gates = scratch("gates_dram", (NT, P, 2 * D))
    with nc.Block() as block:
        @block.sync
        def _(sp):
            stream(sp, "w_in")

        @block.tensor
        def _(t):
            dense(t, "w_in", 11, 16, X_)
            chunks[0] += 11
            for tt in range(NT):
                t.wait_ge(S(f"psum_free{tt}"), 11)
            dense(t, "w_in", 8, 16, X_, at=11)
            chunks[0] -= 11

        @block.vector
        def _(v):
            evac(v, split_lo, "w_in", 11, 16, [0], to(PR)(v, False), last=False)
            evac(v, split_lo, "w_in", 8, 16, [], None, at=11, first=False)

        @block.scalar
        def _(a):
            evac(a, split_hi, "w_in", 11, 16, [1], to(PR)(a, True), last=False)

            def gate(tt, bank, c, par):
                return a.activation(gstage[:, par, tt, :], bank, ACT.Sigmoid)

            def gate_out(j, c):
                a.drain()
                a.dma_start(gates[:, :, ds(j * 1024 + c * 512, 512)].rearrange("t p f -> p t f"),
                            gstage[:, c]).then_inc(S("gate_out"), 16)
                a.wait_ge(S("gate_out"), j * 32 + 16 * (c + 1))
            evac(a, split_hi, "w_in", 8, 16, [0, 1], gate, at=11, first=False, after=gate_out)
    chunks[0] += 19

    keep = bump[0] = base + ((PW * NT * 4 + 31) // 32 * 32)
    oT = sb("oT", (P, 8, T))
    mark = bump[0]
    cn = sb("cn", (P, NT, 256))
    cT = sb("cT", (P, 2, T))
    wuk, wuv = (xT[:, 8 * i:8 * i + 8, :].rearrange("p k c -> p (k c)").rearrange("p (a c) -> p a c", a=2)
                for i in range(2))
    kvg = sb("kvg", (P, 256))
    qT = sb("qT", (P, 8, T))
    kT = sb("kT", (P, 8, T))
    vv = sb("vv", (P, NT, RW))
    iqT = sb("iqT", (P, 4, T))
    ik2 = sb("ik2", (P, NT, P))
    ikT = sb("ikT", (P, T))
    iw = sb("iw", (P, NT, 8))
    relu = sb("relu", (P, 8, T))
    score = sb("score", (P, T))
    work = sb("work", (P, 2, T))
    top8 = sb("top8", (P, 8))
    limit = sb("limit", (P, NT, T))
    pen = sb("pen", (P, NT, T))
    bucket = sb("bucket", (32, 512))
    relb = sb("relb", (32, 16))
    anti = sb("anti", (P, P))
    bline = sb("bline", (16, 512))
    bdram = scratch("bias_dram", (16, 512))
    bias = over("bias", (P, 16, T), F32, spare_at)
    prob = sb("prob", (P, 2, T))
    pn = sb("pn", (P, 2, T))
    pT = sb("pT", (P, 2, 2, P))
    oo = sb("oo", (P, RW))
    st = sb("st", (P, 4, 16))
    with nc.Block() as block:
        @block.sync
        def _(sp):
            for dst, src in ((kvg[:], bcast("kv_norm_g")), (wuk, dram["w_uk"]), (wuv, dram["w_uv"]),
                             (limit[:].rearrange("p t s -> p (t s)"), consts["limit"]),
                             (bucket[:], consts["bucket"][0:32]), (anti[:], consts["anti"]), (relb[:], dram["rel_bias"])):
                sp.dma_start(dst, src).then_inc(S("dsa_in"), 16)
            sp.wait_ge(S("bline"), 1)
            sp.dma_start(bdram, bline[:]).then_inc(S("bline_out"), 16)
            sp.wait_ge(S("bline_out"), 16)
            for tt in range(NT):
                w = P * (tt + 1)
                if tt:
                    sp.wait_ge(S("dsa_tile_done"), 1)
                for h in range(16):
                    sp.dma_start(bias[:, h, 0:w], bass.AP(bdram.tensor, h * 512 + P - P * tt, [[1, P], [1, w]]))\
                        .then_inc(S("bias_in"), 16)

        @block.scalar
        def _(a):
            for tt in range(NT):
                a.activation(relu[:, 0, :], PR[:, tt, C_KV:C_KV + 256], ACT.Square, accum_out=st[:, 0, tt:tt + 1])
                a.drain()
                a.activation(st[:, 1, tt:tt + 1], st[:, 0, tt:tt + 1], ACT.Sqrt, bias=EPS, scale=1.0 / 256)\
                    .then_inc(S("c_sq"), 1)
                a.drain()
            for tt in range(NT):
                a.wait_ge(S("q_turned"), tt + 1)
                a.mul(qT[:, 0:4, tt * P:(tt + 1) * P], PS[:, 0, :].rearrange("p (k c) -> p k c", k=4), SA_SCALE)
                a.mul(qT[:, 4:8, tt * P:(tt + 1) * P], PS[:, 1, :].rearrange("p (k c) -> p k c", k=4), SA_SCALE)
                a.copy(iqT[:, :, tt * P:(tt + 1) * P], PS[:, 2, :].rearrange("p (k c) -> p k c", k=4))
                a.copy(cT[:, :, tt * P:(tt + 1) * P], PS[:, 3, 0:256].rearrange("p (k c) -> p k c", k=2))
                a.copy(ikT[:, tt * P:(tt + 1) * P], PS[:, 4, 0:P])
                a.drain().then_inc(S("q_copied"), 1)
            a.wait_ge(S("kv_ready"), 1)
            a.copy(kT[:, 0:4, :], PS[:, 0:2, :].rearrange("p b (k c) -> p (b k) c", k=2))
            a.copy(kT[:, 4:8, :], PS[:, 2:4, :].rearrange("p b (k c) -> p (b k) c", k=2))
            a.copy(vv[:, 0, :], PS[:, 4:6, :].rearrange("p b c -> p (b c)"))
            a.copy(vv[:, 1, :], PS[:, 6:8, :].rearrange("p b c -> p (b c)"))
            a.drain().then_inc(S("kv_copied"), 1)
            a.wait_ge(S("bline_ps"), 1)
            a.copy(bline[:], PS[0:16, 0, :]).then_inc(S("bline"), 1)
            for tt in range(NT):
                w = P * (tt + 1)
                a.wait_ge(S("idx_ready"), tt + 1)
                for b in range(4):
                    h0 = b // 2 + 4 * (b % 2)
                    a.activation(relu[:, h0:h0 + 3:2, 0:w],
                                 PS[:, b, :].rearrange("p (k c) -> p k c", k=2)[:, :, 0:w], ACT.Relu)
                a.drain().then_inc(S("idx_relu"), 1)
                for h in range(16):
                    n = tt * 16 + h
                    a.wait_ge(S("dsa_max"), n + 1)
                    a.activation(prob[:, h % 2, 0:w], prob[:, h % 2, 0:w], ACT.Exp,
                                 bias=st[:, 2, h:h + 1], accum_out=st[:, 3, h:h + 1]).then_inc(S("dsa_exp"), 1)
                    a.wait_ge(S("pT_ps"), n + 1)
                    if n >= 2:
                        a.wait_ge(S("pv"), n - 1)
                    a.copy(pT[:, h % 2, 0:tt + 1, :], PS[:, 2 + h % 2, 0:w].rearrange("p (k c) -> p k c", c=P))\
                        .then_inc(S("pT_sb"), 1)
                a.wait_ge(S("pv"), 16 * (tt + 1))
                a.copy(oo[:], PS[:, 4:6, :].rearrange("p b c -> p (b c)")).then_inc(S("oo"), 1)
                a.wait_ge(S("o_turned"), tt + 1)
                a.copy(oT[:, :, tt * P:(tt + 1) * P], PS[:, 6:8, :].rearrange("p b (k c) -> p (b k) c", k=4))
                a.drain().then_inc(S("dsa_tile_done"), 1)

        @block.vector
        def _(v):
            v.wait_ge(S("dsa_in"), 112)
            for tt in range(NT):
                v.wait_ge(S("c_sq"), tt + 1)
                v.reciprocal(st[:, 2, tt:tt + 1], st[:, 1, tt:tt + 1])
                v.drain()
                v.scalar_tensor_tensor(out=cn[:, tt, :], in0=PR[:, tt, C_KV:C_KV + 256], scalar=st[:, 2, tt:tt + 1],
                                       in1=kvg[:], op0=ALU.mult, op1=ALU.mult)
                v.tensor_copy(ik2[:, tt, :].rearrange("p (a c) -> p a c", a=2),
                              PR[:, tt, C_IK:C_IK + 64].unsqueeze(1).broadcast_to((P, 2, 64)))
                v.tensor_scalar(iw[:, tt, :], PR[:, tt, C_IW:C_IW + 8], IDX_SCALE, None, ALU.mult)
                v.drain().then_inc(S("c_norm"), 1)
            for tt in range(NT):
                w = P * (tt + 1)
                v.wait_ge(S("idx_relu"), tt + 1)
                v.tensor_scalar(score[:, 0:w], relu[:, 0, 0:w], iw[:, tt, 0:1], None, ALU.mult)
                for h in range(1, 8):
                    v.drain()
                    v.scalar_tensor_tensor(out=score[:, 0:w], in0=relu[:, h, 0:w], scalar=iw[:, tt, h:h + 1],
                                           in1=score[:, 0:w], op0=ALU.mult, op1=ALU.add)
                v.drain()
                v.tensor_tensor(work[:, 0, 0:w], score[:, 0:w], limit[:, tt, 0:w], ALU.min)
                v.drain()
                for r in range(TOPK // 8):
                    v.max(top8[:], work[:, r % 2, 0:w])
                    v.drain()
                    v.match_replace(out=work[:, (r + 1) % 2, 0:w], in_to_replace=top8[:], in_values=work[:, r % 2, 0:w],
                                    imm_value=TAKEN)
                    v.drain()
                v.tensor_scalar(pen[:, tt, 0:w], work[:, 0, 0:w], TAKEN, -NEG, ALU.is_equal, ALU.mult)
                v.drain()
                v.tensor_scalar(pen[:, tt, 0:w], pen[:, tt, 0:w], NEG, None, ALU.add)
                v.drain()
                for h in range(16):
                    n = tt * 16 + h
                    v.wait_ge(S("qk"), n + 1)
                    if n >= 2:
                        v.wait_ge(S("dsa_norm_read"), n - 1)
                    v.tensor_tensor(prob[:, h % 2, 0:w], PS[:, h % 2, 0:w], pen[:, tt, 0:w], ALU.add)
                    v.drain().then_inc(S("qk_read"), 1)
                    v.tensor_reduce(st[:, 1, h:h + 1], prob[:, h % 2, 0:w], X, ALU.max)
                    v.drain()
                    v.tensor_scalar(st[:, 2, h:h + 1], st[:, 1, h:h + 1], -1.0, None, ALU.mult).then_inc(S("dsa_max"), 1)
                    v.wait_ge(S("dsa_exp"), n + 1)
                    v.reciprocal(st[:, 1, h:h + 1], st[:, 3, h:h + 1])
                    v.drain()
                    if n >= 2:
                        v.wait_ge(S("pT_ps"), n - 1)
                    v.tensor_scalar(pn[:, h % 2, 0:w], prob[:, h % 2, 0:w], st[:, 1, h:h + 1], None, ALU.mult)\
                        .then_inc(S("dsa_norm"), 1)
                    v.drain().then_inc(S("dsa_norm_read"), 1)

        @block.tensor
        def _(t):
            for tt in range(NT):
                t.wait_ge(S("c_norm"), tt + 1)
                if tt:
                    t.wait_ge(S("q_copied"), tt)
                for k in range(8):
                    nc.tensor.transpose(PS[:, k // 4, (k % 4) * P:(k % 4 + 1) * P],
                                        PR[:, tt, C_Q + k * P:C_Q + (k + 1) * P], ident[:])
                for k in range(4):
                    nc.tensor.transpose(PS[:, 2, k * P:(k + 1) * P], PR[:, tt, C_IQ + k * P:C_IQ + (k + 1) * P], ident[:])
                for k in range(2):
                    nc.tensor.transpose(PS[:, 3, k * P:(k + 1) * P], cn[:, tt, k * P:(k + 1) * P], ident[:])
                nc.tensor.transpose(PS[:, 4, 0:P], ik2[:, tt, :], ident[:]).then_inc(S("q_turned"), 1)
            t.wait_ge(S("q_copied"), 2)
            t.wait_ge(S("dsa_in"), 112)
            for pr in range(8):
                for r in range(2):
                    nc.tensor.matmul(PS[:, pr // 2, (pr % 2) * T:(pr % 2 + 1) * T], wuk[:, r, pr * P:(pr + 1) * P],
                                     cT[:, r, :], start=(r == 0), stop=(r == 1))
            for tt in range(NT):
                for hf in range(2):
                    for r in range(2):
                        mm = nc.tensor.matmul(PS[:, 4 + 2 * tt + hf, :], cT[:, r, tt * P:(tt + 1) * P],
                                              wuv[:, r, hf * 512:(hf + 1) * 512], start=(r == 0), stop=(r == 1))
            mm.then_inc(S("kv_ready"), 1)
            t.wait_ge(S("kv_copied"), 1)
            nc.tensor.matmul(PS[0:16, 0, :], relb[:], bucket[:], start=True, stop=True).then_inc(S("bline_ps"), 1)
            t.wait_ge(S("bline"), 1)
            for tt in range(NT):
                w = P * (tt + 1)
                if tt:
                    t.wait_ge(S("dsa_tile_done"), tt)
                for h in range(8):
                    r = slice(64 * (h % 2), 64 * (h % 2) + 64)
                    bk, sl = 2 * (h % 2) + h // 4, h // 2 % 2
                    mm = nc.tensor.matmul(PS[:, bk, sl * T:sl * T + w], iqT[r, h // 2, tt * P:(tt + 1) * P],
                                          ikT[r, 0:w], start=True, stop=True)
                mm.then_inc(S("idx_ready"), 1)
                t.wait_ge(S("idx_relu"), tt + 1)

                def qk(h):
                    n = tt * 16 + h
                    if n >= 2:
                        t.wait_ge(S("qk_read"), n - 1)
                    r = slice(64 * (h % 2), 64 * (h % 2) + 64)
                    nc.tensor.matmul(PS[:, h % 2, 0:w], anti[:], bias[:, h, 0:w], start=True, stop=False)
                    nc.tensor.matmul(PS[:, h % 2, 0:w], qT[r, h // 2, tt * P:(tt + 1) * P], kT[r, h // 2, 0:w],
                                     start=False, stop=True).then_inc(S("qk"), 1)
                t.wait_ge(S("bias_in"), 256 * (tt + 1))
                qk(0)
                for h in range(16):
                    n = tt * 16 + h
                    if h + 1 < 16:
                        qk(h + 1)
                    t.wait_ge(S("dsa_norm"), n + 1)
                    if n >= 2:
                        t.wait_ge(S("pT_sb"), n - 1)
                    for k in range(tt + 1):
                        mm = nc.tensor.transpose(PS[:, 2 + h % 2, k * P:(k + 1) * P], pn[:, h % 2, k * P:(k + 1) * P], ident[:])
                    mm.then_inc(S("pT_ps"), 1)
                    t.wait_ge(S("pT_sb"), n + 1)
                    for k in range(tt + 1):
                        mm = nc.tensor.matmul(PS[:, 4 + h // 8, (h % 8) * 64:(h % 8 + 1) * 64], pT[:, h % 2, k, :],
                                              vv[:, k, h * 64:(h + 1) * 64], start=(k == 0), stop=(k == tt))
                    mm.then_inc(S("pv"), 1)
                t.wait_ge(S("oo"), tt + 1)
                for k in range(8):
                    mm = nc.tensor.transpose(PS[:, 6 + k // 4, (k % 4) * P:(k % 4 + 1) * P], oo[:, k * P:(k + 1) * P], ident[:])
                mm.then_inc(S("o_turned"), 1)


    bump[0] = mark
    prev = sb("prev", (P, NT, RW_IN))
    mix = sb("mix", (P, RW_IN))
    with nc.Block() as block:
        @block.gpsimd
        def _(g):
            g.dma_start(mix[:], bcast("shift_mix")).then_inc(S("mix_in"), 16)
            g.memset(prev[0:1, 0, :], 0.0).then_inc(S("prev0"), 1)
            g.dma_start(prev[1:P, 0, :], PR[0:P - 1, 0, 0:RW_IN]).then_inc(S("prev_in"), 16)
            g.dma_start(prev[1:P, 1, :], PR[0:P - 1, 1, 0:RW_IN]).then_inc(S("prev_in"), 16)
            g.dma_start(prev[0:1, 1, :], PR[P - 1:P, 0, 0:RW_IN]).then_inc(S("prev_in"), 16)

        @block.vector
        def _(v):
            v.wait_ge(S("mix_in"), 16)
            v.wait_ge(S("prev0"), 1)
            v.wait_ge(S("prev_in"), 48)
            z = PR[:, :, 0:RW_IN]
            v.tensor_tensor(prev[:], prev[:], z, ALU.subtract)
            v.drain()
            v.tensor_tensor(prev[:], prev[:], mix[:].unsqueeze(1).broadcast_to((P, NT, RW_IN)), ALU.mult)
            v.drain()
            v.tensor_tensor(PR[:, :, C_ZS:RW_IN], PR[:, :, C_ZS:RW_IN], prev[:, :, C_ZS:], ALU.add)
            v.drain().then_inc(S("zs"), 1)
            v.tensor_tensor(PR[:, :, 0:C_ZS], PR[:, :, 0:C_ZS], prev[:, :, 0:C_ZS], ALU.add)

        @block.scalar
        def _(a):
            a.wait_ge(S("zs"), 1)
            a.activation(PR[:, :, C_ZS:C_ZS + 64], PR[:, :, C_ZS:C_ZS + 64], ACT.Tanh)
            a.activation(PR[:, :, C_ZS + 128:C_ZS + 288], PR[:, :, C_ZS + 128:C_ZS + 288], ACT.Sigmoid)
            a.drain().then_inc(S("zs_act"), 1)

    bump[0] = mark
    HC = 512
    NH = 8
    spare = [PR[:, tt, C_Q:C_Q + 2048] for tt in range(NT)]
    AT = spare[0][:, 0:1024].rearrange("p (q a c) -> p q a c", q=4, a=2)
    BK = spare[0][:, 1024:2048].rearrange("p (q a c) -> p q a c", q=4, a=2)
    up = spare[1][:, 0:512]
    gup1 = spare[1][:, 512:1024]
    gup2 = spare[1][0:32, 1024:1536]
    zT = spare[1][:, 1536:1792].rearrange("p (t c) -> p t c", t=NT)
    zgT = spare[1][:, 1792:2048].rearrange("p (t c) -> p t c", t=NT)
    LM = x[:].rearrange("p t d -> p (t d)").rearrange("p (h m c) -> p h m c", h=NH, m=4)
    FT = xT[0:64, 0:8, :].rearrange("p k c -> p (k c)").rearrange("p (c h k) -> p c h k", c=NCH, h=NH)
    Hs = xT[0:64, 8:16, :].rearrange("p k c -> p (k c)").rearrange("p (c h k) -> p c h k", c=NCH, h=NH)
    zgT2 = sb("zgT2", (32, NT, P))
    par = over("par", (P, 7, HC), F32, spare_at)
    w0_, a0_, kk_, ka_, rk_, lw_, lb_ = (par[:, i, :] for i in range(7))
    tmp7 = {n: sb("rw_" + n, (P, HC)) for n in ("sg", "a", "gt", "kk", "k4", "b", "t1", "Ei", "En", "Ee", "Es", "bt", "v", "y")}
    sg, aa, gt, kk, k4, bb, t1, Ei, En, Ee, Es, bt, vb, yy = (tmp7[n] for n in tmp7)
    h3 = lambda ap: ap[:].rearrange("p (h c) -> p h c", h=NH)
    s8 = sb("s8", (P, 4, NH))
    per_head = lambda i: s8[:, i, :].unsqueeze(2).broadcast_to((P, NH, HD))
    PC = sb("PC", (64, NH, NCH))
    TT = sb("TT", (P, NH, P))
    Lp = sb("Lp", (P, CH, CH))
    Xs = sb("Xs", (P, 8, CH))
    X0 = sb("X0", (P, 8, CH))
    terms = sb("terms", (P, 8, CH))
    Wm = sb("Wm", (P, HC))
    MV = sb("MV", (P, HC))
    U0 = sb("U0", (P, HC))
    RWT = sb("RWT", (64, NH, P))
    ST = sb("ST", (64, NCH + 1, NH, HD))
    Ld = scratch("L_dram", (NCH, NH, CH, CH))
    Td = scratch("T_dram", (NCH, NH, CH, CH))
    chunk_rows = [slice(CH * c, CH * c + CH) for c in range(NCH)]
    with nc.Block() as block:
        @block.gpsimd
        def _(g):
            g.memset(TT[:], 0.0).then_inc(S("TT_zero"), 1)

        @block.sync
        def _(sp):
            sp.dma_start(X0[:], consts["unit_x"].rearrange("p (j t) -> p j t", j=8)).then_inc(S("X0_in"), 16)
            sp.wait_ge(S("TT_zero"), 1)
            for hf in range(2):
                sp.wait_ge(S("it_done"), hf * 2 + 1)
                for k, n in enumerate(("w0", "a0", "k_k", "k_a", "r_k", "ln_x_w", "ln_x_b")):
                    row = dram[n].rearrange("(a n) -> a n", a=1)
                    sp.dma_start(par[:, k, :], row[:, ds(hf * HC, HC)].broadcast_to((P, HC))).then_inc(S("par_in"), 16)
                sp.dma_start(up, dram["up"][:, ds(hf * HC, HC)]).then_inc(S("par_in"), 16)
                sp.dma_start(gup1, dram["gate_up"][0:P, ds(hf * HC, HC)]).then_inc(S("par_in"), 16)
                sp.dma_start(gup2, dram["gate_up"][P:P + 32, ds(hf * HC, HC)]).then_inc(S("par_in"), 16)
                for i in range(NT):
                    sp.wait_ge(S("LM_sb"), hf * 16 + (8 * i + 8))
                    for c in range(NCH):
                        sp.dma_start(Ld[c].rearrange("h s t -> s h t"), LM[chunk_rows[c], :, 0, chunk_rows[c]])\
                            .then_inc(S("L_out"), 16)
                    sp.wait_ge(S("L_out"), hf * 128 + (64 * i + 64))
                    for q in range(4):
                        sp.dma_start(Lp[chunk_rows[q]], Ld.rearrange("c h s t -> (c h) s t")).then_inc(S("L_in"), 16)
                    sp.wait_ge(S("X_ready"), hf * 2 + (i + 1))
                    for q in range(4):
                        sp.dma_start(Td.rearrange("c h s t -> (c h) s t")[:, 8 * q:8 * q + 8, :], Xs[chunk_rows[q]])\
                            .then_inc(S("T_out"), 16)
                    sp.wait_ge(S("T_out"), hf * 128 + (64 * i + 64))
                    for c in range(NCH):
                        sp.dma_start(TT[chunk_rows[c], :, chunk_rows[c]], Td[c].rearrange("h s t -> s h t"))\
                            .then_inc(S("T_in"), 16)

        @block.scalar
        def _(a):
            a.wait_ge(S("z_turned"), 1)
            a.copy(zT, PS[:, 0, 0:256].rearrange("p (t c) -> p t c", t=NT))
            a.copy(zgT, PS[:, 1, 0:256].rearrange("p (t c) -> p t c", t=NT))
            a.copy(zgT2[:], PS[0:32, 2, 0:256].rearrange("p (t c) -> p t c", t=NT))
            a.drain().then_inc(S("z_T"), 1)
            with a.Fori(0, 2) as hf:
                for i in range(NT):
                    nth = lambda m, k: hf * (2 * m) + (m * i + k)
                    a.wait_ge(S("up_ps"), nth(1, 1))
                    a.copy(gt[:], PS[:, 2, :])
                    a.wait_ge(S("u_sum"), nth(1, 1))
                    a.activation(sg[:], sg[:], ACT.Sigmoid).then_inc(S("sig"), 1)
                    a.activation(aa[:], aa[:], ACT.Sigmoid).then_inc(S("a_sb"), 1)
                    a.wait_ge(S("kk_ss"), nth(1, 1))
                    a.activation(s8[:, 1, :], s8[:, 0, :], ACT.Sqrt).then_inc(S("kk_norm"), 1)
                    a.wait_ge(S("G_ps"), nth(1, 1))
                    a.activation(Ei[:], PS[:, 3, :], ACT.Exp, scale=-DECAY)
                    a.activation(En[:], PS[:, 3, :], ACT.Exp, scale=DECAY)
                    a.activation(Ee[:], PS[:, 4, :], ACT.Exp, scale=-DECAY)
                    a.activation(Es[:], PS[:, 5, :], ACT.Exp, scale=-DECAY)
                    a.activation(PC[:], PS[0:64, 6, 0:32].rearrange("p (h c) -> p h c", h=NH), ACT.Exp, scale=-DECAY)
                    a.drain().then_inc(S("exps"), 1)
                    a.wait_ge(S("turn_ps"), nth(1, 1))
                    for b in range(2):
                        a.copy(AT[:, 2 * b:2 * b + 2, :, :], PS[:, b, :].rearrange("p (q a c) -> p q a c", q=2, a=2))
                    a.drain().then_inc(S("AT_sb"), 1)
                    a.wait_ge(S("MV_ps"), nth(1, 1))
                    a.copy(MV[:], PS[:, 0, :]).then_inc(S("MV_sb"), 1)
                    a.wait_ge(S("WU_ps"), nth(1, 1))
                    a.copy(Wm[:], PS[:, 1, :]).then_inc(S("Wm_sb"), 1)
                    a.wait_ge(S("RW_ps"), nth(1, 1))
                    a.copy(RWT[:, 0:4, :], PS[0:64, 7, :].rearrange("p (h c) -> p h c", h=4))
                    a.copy(RWT[:, 4:8, :], PS[0:64, 0, :].rearrange("p (h c) -> p h c", h=4))
                    a.drain().then_inc(S("RW_sb"), 1)
                    a.wait_ge(S("H_ps"), nth(1, 1))
                    a.copy(Hs, PS[0:64, 1:5, :].rearrange("p c (h k) -> p c h k", h=NH))
                    a.drain().then_inc(S("H_sb"), 1)
                    a.wait_ge(S("Yi_ps"), nth(1, 1))
                    a.copy(yy[:], PS[:, 5, :]).then_inc(S("Yi_sb"), 1)
                    a.wait_ge(S("gn_var"), nth(1, 1))
                    a.activation(s8[:, 1, :], s8[:, 0, :], ACT.Sqrt, bias=GN_EPS, scale=1.0 / HD).then_inc(S("gn_std"), 1)

        @block.vector
        def _(v):
            v.wait_ge(S("X0_in"), 16)
            v.nop().then_inc(S("it_done"), 1)
            with v.Fori(0, 2) as hf:
                for i in range(NT):
                    nth = lambda m, k: hf * (2 * m) + (m * i + k)
                    rv = PR[:, i, ds(hf * HC, HC)]
                    kv = PR[:, i, ds(hf * HC + RW, HC)]
                    vv_ = PR[:, i, ds(hf * HC + 2 * RW, HC)]
                    v.wait_ge(S("par_in"), hf * 160 + 160)
                    v.wait_ge(S("up_ps"), nth(1, 1))
                    v.tensor_tensor(sg[:], PS[:, 0, :], w0_, ALU.add)
                    v.tensor_tensor(aa[:], PS[:, 1, :], a0_, ALU.add)
                    v.drain().then_inc(S("u_sum"), 1)
                    v.tensor_copy(vb[:], vv_)
                    v.tensor_tensor(kk[:], kv, kk_, ALU.mult)
                    v.drain()
                    v.tensor_tensor(t1[:], kk[:], kk[:], ALU.mult)
                    v.drain()
                    v.tensor_reduce(s8[:, 0, :], h3(t1), X, ALU.add).then_inc(S("kk_ss"), 1)
                    v.wait_ge(S("kk_norm"), nth(1, 1))
                    v.tensor_scalar(s8[:, 2, :], s8[:, 1, :], 1e-12, None, ALU.max)
                    v.drain()
                    v.reciprocal(s8[:, 3, :], s8[:, 2, :])
                    v.drain()
                    v.tensor_tensor(h3(kk), h3(kk), per_head(3), ALU.mult)
                    v.wait_ge(S("a_sb"), nth(1, 1))
                    v.scalar_tensor_tensor(out=t1[:], in0=aa[:], scalar=-1.0, in1=ka_, op0=ALU.add, op1=ALU.mult)
                    v.drain()
                    v.scalar_tensor_tensor(out=k4[:], in0=t1[:], scalar=1.0, in1=kv, op0=ALU.add, op1=ALU.mult)
                    v.tensor_tensor(bb[:], kk[:], aa[:], ALU.mult)
                    v.wait_ge(S("exps"), nth(1, 1))
                    v.tensor_tensor(Ei[:], Ei[:], rv, ALU.mult)
                    v.scalar_tensor_tensor(out=Ee[:], in0=kk[:], scalar=-1.0, in1=Ee[:], op0=ALU.mult, op1=ALU.mult)
                    v.drain()
                    v.tensor_tensor(bt[:], bb[:], En[:], ALU.mult)
                    v.drain()
                    v.tensor_tensor(En[:], k4[:], En[:], ALU.mult)
                    v.drain().then_inc(S("prep"), 1)
                    v.tensor_tensor(bb[:], bb[:], Es[:], ALU.mult)
                    v.drain()
                    v.tensor_tensor(Es[:], k4[:], Es[:], ALU.mult)
                    for c in range(NCH):
                        v.tensor_tensor(FT[:, c], ident[0:64, 0:64].unsqueeze(1).broadcast_to((64, NH, 64)),
                                        PC[:, :, c].unsqueeze(2).broadcast_to((64, NH, 64)), ALU.mult)
                    v.wait_ge(S("turn_ps"), nth(1, 1))
                    for b in range(2):
                        v.tensor_copy(BK[:, 2 * b:2 * b + 2, :, :],
                                      PS[:, 2 + b, :].rearrange("p (q a c) -> p q a c", q=2, a=2))
                    v.drain().then_inc(S("BK_sb"), 1)
                    for h in range(NH):
                        v.wait_ge(S("LM_ps"), nth(8, h + 1))
                        v.tensor_tensor(LM[:, h].rearrange("p (b m) c -> p b (m c)", b=2),
                                        PS[:, 4 + h % 4, :].rearrange("p (b m) -> p b m", b=2),
                                        incl3[:, 0:2, :].rearrange("p m c -> p (m c)").unsqueeze(1)
                                        .broadcast_to((P, 2, 256)), ALU.mult)
                        v.drain().then_inc(S("LM_sb"), 1)
                    v.wait_ge(S("L_in"), nth(64, 64))
                    v.memset(Lp[:].rearrange("p s t -> p (s t)")[:, 0:CH * CH:CH + 1], 1.0)
                    v.tensor_copy(Xs[:], X0[:])
                    for t_ in range(1, CH):
                        v.drain()
                        v.tensor_tensor(terms[:, :, 0:t_ + 1], Xs[:, :, 0:t_ + 1],
                                        Lp[:, 0:t_ + 1, t_].unsqueeze(1).broadcast_to((P, 8, t_ + 1)), ALU.mult)
                        v.drain()
                        v.tensor_reduce(Xs[:, :, t_], terms[:, :, 0:t_ + 1], X, ALU.add)
                    v.drain().then_inc(S("X_ready"), 1)
                    v.wait_ge(S("WU_ps"), nth(1, 1))
                    v.tensor_copy(U0[:], PS[:, 2, :]).then_inc(S("U0_sb"), 1)
                    v.wait_ge(S("F_ps"), nth(1, 1))
                    v.tensor_tensor(FT, FT, PS[0:64, 3:7, :].rearrange("p c (h k) -> p c h k", h=NH), ALU.add)
                    v.drain().then_inc(S("F_sb"), 1)
                    if i == 0:
                        v.memset(ST[:, 0], 0.0)
                    else:
                        v.tensor_copy(ST[:, 0], ST[:, NCH])
                    v.drain().then_inc(S("ST_ready"), 1)
                    v.wait_ge(S("H_sb"), nth(1, 1))
                    for c in range(NCH):
                        v.wait_ge(S("ch_ps"), nth(4, c + 1))
                        v.tensor_tensor(ST[:, c + 1], PS[0:64, 6, :].rearrange("p (h k) -> p h k", h=NH), Hs[:, c], ALU.add)
                        v.drain().then_inc(S("ST_ready"), 1)
                    v.wait_ge(S("Yi_sb"), nth(1, 1))
                    v.wait_ge(S("Ys_ps"), nth(1, 1))
                    v.tensor_tensor(yy[:], yy[:], PS[:, 7, :], ALU.add)
                    v.drain()
                    v.tensor_reduce(s8[:, 2, :], h3(yy), X, ALU.add)
                    v.drain()
                    v.tensor_scalar(s8[:, 3, :], s8[:, 2, :], -1.0 / HD, None, ALU.mult)
                    v.drain()
                    v.tensor_tensor(h3(yy), h3(yy), per_head(3), ALU.add)
                    v.drain()
                    v.tensor_tensor(t1[:], yy[:], yy[:], ALU.mult)
                    v.drain()
                    v.tensor_reduce(s8[:, 0, :], h3(t1), X, ALU.add).then_inc(S("gn_var"), 1)
                    v.tensor_tensor(k4[:], k4[:], rv, ALU.mult)
                    v.drain()
                    v.tensor_tensor(k4[:], k4[:], rk_, ALU.mult)
                    v.drain()
                    v.tensor_reduce(s8[:, 2, :], h3(k4), X, ALU.add)
                    v.wait_ge(S("gn_std"), nth(1, 1))
                    v.reciprocal(s8[:, 3, :], s8[:, 1, :])
                    v.drain()
                    v.tensor_tensor(h3(yy), h3(yy), per_head(3), ALU.mult)
                    v.drain()
                    v.tensor_tensor(yy[:], yy[:], lw_, ALU.mult)
                    v.tensor_tensor(h3(t1), h3(vb), per_head(2), ALU.mult)
                    v.drain()
                    v.tensor_tensor(yy[:], yy[:], lb_, ALU.add)
                    v.drain()
                    v.tensor_tensor(yy[:], yy[:], t1[:], ALU.add)
                    v.drain()
                    v.tensor_tensor(rv, yy[:], gt[:], ALU.mult)
                    v.drain().then_inc(S("it_done"), 1)

        @block.tensor
        def _(t):
            mm_ = nc.tensor.matmul
            for tt in range(NT):
                cs = slice(tt * P, (tt + 1) * P)
                nc.tensor.transpose(PS[:, 0, cs], PR[:, tt, C_ZS:C_ZS + P], ident[:])
                nc.tensor.transpose(PS[:, 1, cs], PR[:, tt, C_ZS + P:C_ZS + 2 * P], ident[:])
                m = nc.tensor.transpose(PS[0:32, 2, cs], PR[:, tt, C_ZS + 2 * P:C_ZS + 288], ident[:])
            m.then_inc(S("z_turned"), 1)
            t.wait_ge(S("z_T"), 1)
            for hf in range(2):
                for i in range(NT):
                    nth = lambda m, k: hf * (2 * m) + (m * i + k)
                    hs = [slice(h * HD, (h + 1) * HD) for h in range(NH)]
                    t.wait_ge(S("it_done"), nth(1, 1))
                    t.wait_ge(S("par_in"), hf * 160 + 160)
                    mm_(PS[:, 0, :], zT[0:64, i, :], up[0:64, :], start=True, stop=True)
                    mm_(PS[:, 1, :], zT[64:P, i, :], up[64:P, :], start=True, stop=True)
                    mm_(PS[:, 2, :], zgT[:, i, :], gup1, start=True, stop=False)
                    mm_(PS[:, 2, :], zgT2[:, i, :], gup2, start=False, stop=True).then_inc(S("up_ps"), 1)
                    t.wait_ge(S("sig"), nth(1, 1))
                    mm_(PS[:, 3, :], incl3[:, 1, :], sg[:], start=True, stop=True)
                    mm_(PS[:, 4, :], incl3[:, 0, :], sg[:], start=True, stop=True)
                    mm_(PS[:, 5, :], incl3[:, 2, :], sg[:], start=True, stop=True)
                    for h in range(NH):
                        m = mm_(PS[0:64, 6, h * NCH:(h + 1) * NCH], sg[:, hs[h]], chunk[:], start=True, stop=True)
                    m.then_inc(S("G_ps"), 1)
                    t.wait_ge(S("prep"), nth(1, 1))
                    for q in range(4):
                        for k, src in enumerate((Ee, Ei, bt, En)):
                            col = (q % 2) * 256 + (k % 2) * P
                            m = nc.tensor.transpose(PS[:, 2 * (k // 2) + q // 2, col:col + P],
                                                    src[:, q * P:(q + 1) * P], ident[:])
                    m.then_inc(S("turn_ps"), 1)
                    t.wait_ge(S("AT_sb"), nth(1, 1))
                    t.wait_ge(S("BK_sb"), nth(1, 1))
                    for h in range(NH):
                        if h >= 4:
                            t.wait_ge(S("LM_sb"), nth(8, h - 3))
                        r = slice(64 * (h % 2), 64 * (h % 2) + 64)
                        rhs = AT[r, h // 2].rearrange("p a c -> p (a c)")
                        mm_(PS[:, 4 + h % 4, 0:256], BK[r, h // 2, 0, :], rhs, start=True, stop=True)
                        mm_(PS[:, 4 + h % 4, 256:512], BK[r, h // 2, 1, :], rhs, start=True, stop=True)\
                            .then_inc(S("LM_ps"), 1)
                    t.wait_ge(S("LM_sb"), nth(8, 8))
                    for h in range(NH):
                        m = mm_(PS[:, 0, hs[h]], LM[:, h, 2, :], vb[:, hs[h]], start=True, stop=True)
                    m.then_inc(S("MV_ps"), 1)
                    t.wait_ge(S("MV_sb"), nth(1, 1))
                    t.wait_ge(S("T_in"), nth(64, 64))
                    for h in range(NH):
                        mm_(PS[:, 1, hs[h]], TT[:, h, :], Ee[:, hs[h]], start=True, stop=True)
                        m = mm_(PS[:, 2, hs[h]], TT[:, h, :], MV[:, hs[h]], start=True, stop=True)
                    m.then_inc(S("WU_ps"), 1)
                    t.wait_ge(S("Wm_sb"), nth(1, 1))
                    for h in range(NH):
                        for c, r in enumerate(chunk_rows):
                            m = mm_(PS[0:64, 3 + c, hs[h]], Wm[r, hs[h]], bb[r, hs[h]], start=True, stop=True)
                    m.then_inc(S("F_ps"), 1)
                    for h in range(NH):
                        o = PS[0:64, 7 if h < 4 else 0, (h % 4) * P:(h % 4 + 1) * P]
                        mm_(o, Ei[:, hs[h]], ident[:], start=True, stop=False)
                        m = mm_(o, Wm[:, hs[h]], LM[:, h, 1, :], start=False, stop=True)
                    m.then_inc(S("RW_ps"), 1)
                    t.wait_ge(S("U0_sb"), nth(1, 1))
                    t.wait_ge(S("F_sb"), nth(1, 1))
                    for h in range(NH):
                        for c, r in enumerate(chunk_rows):
                            mm_(PS[0:64, 1 + c, hs[h]], bb[r, hs[h]], U0[r, hs[h]], start=True, stop=False)
                            m = mm_(PS[0:64, 1 + c, hs[h]], Es[r, hs[h]], vb[r, hs[h]], start=False, stop=True)
                    m.then_inc(S("H_ps"), 1)
                    for h in range(NH):
                        mm_(PS[:, 5, hs[h]], LM[:, h, 1, :], U0[:, hs[h]], start=True, stop=False)
                        m = mm_(PS[:, 5, hs[h]], LM[:, h, 3, :], vb[:, hs[h]], start=False, stop=True)
                    m.then_inc(S("Yi_ps"), 1)
                    t.wait_ge(S("RW_sb"), nth(1, 1))
                    for c, r in enumerate(chunk_rows):
                        t.wait_ge(S("ST_ready"), nth(5, c + 1))
                        for h in range(NH):
                            m = mm_(PS[0:64, 6, hs[h]], FT[:, c, h, :], ST[:, c, h, :], start=True, stop=True)
                        m.then_inc(S("ch_ps"), 1)
                        for h in range(NH):
                            m = mm_(PS[r, 7, hs[h]], RWT[:, h, r], ST[:, c, h, :], start=True, stop=True)
                    m.then_inc(S("Ys_ps"), 1)

    recycle()

    bump[0] = mark
    yaT = sb("yaT", (P, 8, T))
    lo_ya = over("lo_ya", (P, 8, T), F32R, mark)
    lo_o = over("lo_o", (P, 8, T), F32R, keep)
    mixed = over("mixed", (P, NT, D), F32, base)
    gsb = sb("gsb", (P, NT, 2 * D))
    with nc.Block() as block:
        @block.sync
        def _(sp):
            sp.dma_start(gsb[:], gates.rearrange("t p f -> p t f")).then_inc(S("gates_back"), 16)
            sp.dma_start(x[:], dram["x"].rearrange("(t p) d -> p t d", p=P)).then_inc(S("x_back"), 16)
            stream(sp, "br_a")
            stream(sp, "br_b")
            sp.wait_ge(S("x_back"), 16)

        @block.tensor
        def _(t):
            for tt in range(NT):
                for k in range(8):
                    m = nc.tensor.transpose(PS[:, 4 + 2 * tt + k // 4, (k % 4) * P:(k % 4 + 1) * P],
                                            PR[:, tt, k * P:(k + 1) * P], ident[:])
                m.then_inc(S("ya_ps"), 1)
            t.wait_ge(S("br_lo"), 1)
            dense(t, "br_a", 4, 8, (hi_x[:, 0:8], lo_ya))
            chunks[0] += 4
            for tt in range(NT):
                t.wait_ge(S(f"psum_free{tt}"), chunks[0])
            dense(t, "br_b", 4, 8, (hi_x[:, 8:16], lo_o))
            chunks[0] -= 4

        @block.scalar
        def _(a):
            for tt in range(NT):
                a.wait_ge(S("ya_ps"), tt + 1)
                a.copy(yaT[:, :, tt * P:(tt + 1) * P], PS[:, 4 + 2 * tt:6 + 2 * tt, :].rearrange("p b (k c) -> p (b k) c", k=4))
            a.drain()
            a.copy(hi_x[:, 0:8], yaT[:])
            a.copy(hi_x[:, 8:16], oT[:])
            a.drain().then_inc(S("br_hi"), 1)
            evac(a, split_hi, "br_a", 4, 8, [], None, last=False)
            evac(a, split_hi, "br_b", 4, 8, [], None, first=False)

        @block.vector
        def _(v):
            v.wait_ge(S("br_hi"), 1)
            v.tensor_tensor(lo_ya[:], yaT[:], hi_x[:, 0:8].bitcast(F32), ALU.subtract)
            v.tensor_tensor(lo_o[:], oT[:], hi_x[:, 8:16].bitcast(F32), ALU.subtract).then_inc(S("br_lo"), 1)
            begin(v, split_lo, "br_a", 8)
            v.wait_ge(S("gates_back"), 16)

            def gated_a(tt, bank, c, par):
                return v.tensor_tensor(mixed[:, tt, ds(c * 512, 512)], bank, gsb[:, tt, ds(c * 512, 512)], ALU.mult)

            def gated_b(tt, bank, c, par):
                g_ = gsb[:, tt, ds(c * 512 + D, 512)]
                v.tensor_tensor(g_, bank, g_, ALU.mult)
                v.drain()
                m_ = mixed[:, tt, ds(c * 512, 512)]
                return v.tensor_tensor(m_, m_, g_, ALU.add)
            evac(v, split_lo, "br_a", 4, 8, [0, 1], gated_a, first=False, last=False)
            evac(v, split_lo, "br_b", 4, 8, [0, 1], gated_b, first=False)
    chunks[0] += 8

    def turn(src):
        i = turns[0]
        turns[0] += 1
        with nc.Block() as block:
            @block.tensor
            def _(t):
                for b in range(8):
                    for k in range(4):
                        kk = (b % 4) * 4 + k
                        m = nc.tensor.transpose(PS[:, b, k * P:(k + 1) * P], src[:, b // 4, kk * P:(kk + 1) * P], ident[:])
                    m.then_inc(S("turned"), 1)

            def copies(e, f):
                for b in range(8):
                    e.wait_ge(S("turned"), 8 * i + b + 1)
                    r, c = part(b)
                    f(b, r, c, PS[:, b, :].rearrange("p (k c) -> p k c", k=4))

            @block.scalar
            def _(a):
                def hi(b, r, c, bank):
                    a.copy(hi_x[:, r, c], bank).then_inc(S("turn_hi"), 1)
                copies(a, hi)

            @block.vector
            def _(v):
                def lo(b, r, c, bank):
                    v.wait_ge(S("turn_hi"), 8 * i + b + 1)
                    v.tensor_tensor(lo_x[:, r, c], bank, hi_x[:, r, c].bitcast(F32), ALU.subtract)
                copies(v, lo)

    def project_residual(name):
        with nc.Block() as block:
            @block.sync
            def _(sp):
                stream(sp, name)

            @block.tensor
            def _(t):
                dense(t, name, 4, 16, X_)

            @block.scalar
            def _(a):
                evac(a, split_hi, name, 4, 16, [], None)

            @block.vector
            def _(v):
                def add(tt, bank, c, par):
                    o = x[:, tt, ds(c * 512, 512)]
                    return v.tensor_tensor(o, o, bank, ALU.add)
                evac(v, split_lo, name, 4, 16, [0, 1], add)
        chunks[0] += 4

    turn(mixed)
    project_residual("w_out")

    norm_T("norm_ffn_g")
    R3 = sb("R3", (P, 3, T))
    iota = sb("iota", (P, P))
    HK = PK // 2
    hot1 = sb("hot1", (P, 2, 8, P))
    hot2 = sb("hot2", (P, 2, 8, HK))
    after_r3 = bump[0]
    GG = sb("GG", (P, T, HK))
    Q = over("Q", (P, NT, D), F32, after_r3)
    qT_ = over("qT_", (P, KC, T), F32, after_r3 + NT * D * 4)
    small_at = bump[0]
    sk = hot1.rearrange("p a q c -> p (a q) c")
    sc = x[:].rearrange("p t (k n) -> p t k n", n=PK)
    x_saved = scratch("x_dram", (P, NT, D))
    w16 = sb("w16", (P, T))
    vals = sb("vals", (P, KC, PT))
    idx = sb("idx", (P, KC, PT), U32)
    idf = sb("idf", (P, KC, PT))
    cand = hot1.rearrange("p a q c -> p (a q c)").rearrange("p (h a b) -> p h a b", h=PH, a=PT)
    tops = sb("tops", (P, PH, PT))
    pos = sb("pos", (P, PH, PT), U32)
    pp = sb("pp", (P, 2, PH, PT), U32)
    ppf = sb("ppf", (P, 2, PH, PT))
    oneh = cand
    route = sb("route", (P, NT, 3, PH, PT))
    zsum = sb("zsum", (P, 2, PH))
    NG = HK // SLOTS
    gg = lambda i: GG[:, :, ds(i, 1)].rearrange("p n i -> p (n i)")

    def units(eng, split, g0, step, lead=0, stops=(), at_stop=None):
        def group(g, more):
            for s in range(SLOTS):
                if step:
                    if s + lead < SLOTS:
                        step(g, s + lead)
                    elif more:
                        step(g + 1, s + lead - SLOTS)
                if s == 0:
                    split(eng, g + g0, SLOTS - 1)
                elif more:
                    split(eng, g + (g0 + 1), s - 1)
        for s in range(lead):
            step(0, s)
        for s in range(SLOTS - 1):
            split(eng, g0, s)
        a = 0
        for i, b in enumerate((*stops, NG - 1)):
            with eng.Fori(a, b) as g:
                group(g, True)
            if i < len(stops):
                at_stop(i)
            a = b
        group(NG - 1, False)

    def inputs(t, hf):
        with t.Fori(0, NG) as g:
            for s in range(SLOTS):
                t.wait_ge(S("gelu_free"), g * 4 + (hf * HK + s + 1))
                t.wait_ge(S(f"lo{s}"), g + (GROUP[f"u{hf}"] + 1))
                for k in range(KC):
                    for p, (wa, xa) in enumerate(((hi_w, hi_x), (hi_w, lo_x), (lo_w, hi_x))):
                        m = nc.tensor.matmul(PS[:, s, 0:T], wa[s][:, k * P:(k + 1) * P], xa[:, k, :],
                                             start=(k == 0 and p == 0), stop=(k == KC - 1 and p == 2))
                m.then_inc(S("unit_used"), 1)

    def gelu(a, hf):
        def step(g, s):
            a.wait_ge(S("unit_used"), g * 4 + (4 * GROUP[f"u{hf}"] + s + 1))
            a.activation(gg(g * 4 + s), PS[:, s, 0:T], ACT.Gelu).then_inc(S("gelu_free"), 1)
        return step

    def top_exp(a, tt):
        a.wait_ge(S("top_diff"), tt + 1)
        a.activation(route[:, tt, 2], route[:, tt, 2], ACT.Exp).then_inc(S("top_exp"), 1)

    with nc.Block() as block:
        @block.sync
        def _(sp):
            sp.dma_start(sk[:], dram["sub_keys"].rearrange("q h c n -> q (h c) n")).then_inc(S("sk_in"), 16)
            cload(sp, iota[:], "iota", S("sk_in"))
            sp.dma_start(x_saved, x[:]).then_inc(S("x_out"), 16)
            stream(sp, "wq")
            stream(sp, "u0")

        @block.tensor
        def _(t):
            dense(t, "wq", 4, 16, X_)
            t.wait_ge(S("sk_in"), 32)
            for tt in range(NT):
                t.wait_ge(S("psum_free0"), chunks[0] + 4)
                t.wait_ge(S("psum_free1"), chunks[0] + 4)
                if tt:
                    t.wait_ge(S("sc_sb"), 1)
                for k in range(KC):
                    m = nc.tensor.transpose(PS[:, 4 + k // 4, (k % 4) * P:(k % 4 + 1) * P], Q[:, tt, k * P:(k + 1) * P], ident[:])
                m.then_inc(S("pq_ps"), 1)
                t.wait_ge(S("pq_sb"), tt + 1)
                for k in range(KC):
                    m = nc.tensor.matmul(PS[:, k // 4, (k % 4) * P:(k % 4 + 1) * P], qT_[:, k, tt * P:(tt + 1) * P], sk[:, k, :],
                                         start=True, stop=True)
                m.then_inc(S("sc_ps"), 1)
            inputs(t, 0)
            for tt in range(NT):
                t.wait_ge(S("route"), tt + 1)
                for k in range(3):
                    m = nc.tensor.transpose(PS[:, 4 + tt, k * P:(k + 1) * P], route[:, tt, k].rearrange("p h k -> p (h k)"), ident[:])
                m.then_inc(S("route_ps"), 1)

        @block.scalar
        def _(a):
            evac(a, split_hi, "wq", 4, 16, [1], to(Q)(a, True))
            for tt in range(NT):
                a.wait_ge(S("pq_ps"), tt + 1)
                a.copy(qT_[:, :, tt * P:(tt + 1) * P], PS[:, 4:8, :].rearrange("p b (k c) -> p (b k) c", k=4))
                a.drain().then_inc(S("pq_sb"), 1)
                a.wait_ge(S("sc_ps"), tt + 1)
                a.wait_ge(S("x_out"), 16)
                a.copy(sc[:, tt].rearrange("p k n -> p (k n)"), PS[:, 0:4, :].rearrange("p b c -> p (b c)"))
                a.drain().then_inc(S("sc_sb"), 1)
            a.nop().then_inc(S("gelu_free"), 4)
            units(a, split_hi, GROUP["u0"], gelu(a, 0), stops=(NG // 4, NG // 2), at_stop=lambda tt: top_exp(a, tt))
            for tt in range(NT):
                a.wait_ge(S("route_ps"), tt + 1)
                a.copy(R3[:, :, tt * P:(tt + 1) * P], PS[:, 4 + tt, 0:3 * P].rearrange("p (k c) -> p k c", k=3))

        @block.gpsimd
        def _(g):
            units(g, split_lo, GROUP["u0"], None)

        @block.vector
        def _(v):
            evac(v, split_lo, "wq", 4, 16, [0], to(Q)(v, False))
            v.wait_ge(S("sk_in"), 32)

            def top16(out, ind, src, w):
                v.max(out[:, 0:8], src)
                v.drain()
                v.match_replace(out=w, in_to_replace=out[:, 0:8], in_values=src, imm_value=NEG)
                v.max_index(ind[:, 0:8], out[:, 0:8], src)
                v.drain()
                v.max(out[:, 8:16], w)
                v.drain()
                v.max_index(ind[:, 8:16], out[:, 8:16], w)

            for tt in range(NT):
                v.wait_ge(S("sc_sb"), tt + 1)
                for k in range(KC):
                    top16(vals[:, k, :], idx[:, k, :], sc[:, tt, k, :], w16[:, 0:P])
                v.drain()
                v.tensor_copy(idf[:], idx[:])
                v2 = vals[:].rearrange("p (h c) k -> p h c k", c=2)
                i2 = idf[:].rearrange("p (h c) k -> p h c k", c=2)
                v.wait_ge(S("sc_sb"), 2)
                v.tensor_tensor(cand, v2[:, :, 0, :].unsqueeze(3).broadcast_to((P, PH, PT, PT)),
                                v2[:, :, 1, :].unsqueeze(2).broadcast_to((P, PH, PT, PT)), ALU.add)
                v.drain()
                for h in range(PH):
                    top16(tops[:, h, :], pos[:, h, :], cand[:, h].rearrange("p a b -> p (a b)"), w16[:])
                v.drain()
                v.tensor_tensor(route[:, tt, 2], tops[:], tops[:, :, 0:1].broadcast_to((P, PH, PT)), ALU.subtract)
                v.drain().then_inc(S("top_diff"), 1)
                v.tensor_scalar(pp[:, 0], pos[:], 4, None, ALU.logical_shift_right)
                v.tensor_scalar(pp[:, 1], pos[:], 15, None, ALU.bitwise_and)
                v.drain()
                v.tensor_copy(ppf[:], pp[:])
                for c in range(2):
                    v.drain()
                    v.tensor_tensor(oneh, ppf[:, c].unsqueeze(3).broadcast_to((P, PH, PT, PT)),
                                    iota[:, 0:PT].unsqueeze(1).unsqueeze(1).broadcast_to((P, PH, PT, PT)), ALU.is_equal)
                    v.drain()
                    v.tensor_tensor(oneh, oneh, i2[:, :, c, :].unsqueeze(2).broadcast_to((P, PH, PT, PT)), ALU.mult)
                    v.drain()
                    v.tensor_reduce(route[:, tt, c], oneh, X, ALU.add)
                v.wait_ge(S("top_exp"), tt + 1)
                v.tensor_reduce(zsum[:, 0, :], route[:, tt, 2], X, ALU.add)
                v.drain()
                v.reciprocal(zsum[:, 1, :], zsum[:, 0, :])
                v.drain()
                v.tensor_tensor(route[:, tt, 2], route[:, tt, 2], zsum[:, 1, :].unsqueeze(2).broadcast_to((P, PH, PT)), ALU.mult)
                v.drain().then_inc(S("route"), 1)
    chunks[0] += 4

    bump[0] = small_at
    hi_g = over("hi_g", (P, SLOTS, T), F32R, bump[0])
    bump[0] += SLOTS * T * 4
    lo_g = over("lo_g", (P, SLOTS, T), F32R, bump[0])
    bump[0] += SLOTS * T * 4
    assert bump[0] <= hi_base

    def peer_half(hf):
        halves = (f"u{hf}", f"v{hf}")
        U, V = (GROUP[n] for n in halves)
        before = hf * T // 8
        if hf:
            with nc.Block() as block:
                @block.sync
                def _(sp):
                    stream(sp, halves[0])

                @block.tensor
                def _(t):
                    inputs(t, hf)

                @block.scalar
                def _(a):
                    units(a, split_hi, U, gelu(a, hf))

                @block.vector
                def _(v):
                    units(v, split_lo, U, None)

        with nc.Block() as block:
            @block.vector
            def _(v):
                wide = lambda ap, n: ap.unsqueeze(2).broadcast_to((P, 8, n))
                if hf == 0:
                    v.nop().then_inc(S("G_read"), 2)

                def product(j, c, k):
                    v.wait_ge(S("G_free"), j * 2 + (before + c + 3))
                    o = GG[:, ds(j * 16 + 8 * c, 8), :].rearrange("p n i -> p (n i)")
                    v.tensor_tensor(o, o, PS[:, k, :], ALU.mult).then_inc(S("G_read"), 1)

                def rows(j, c):
                    v.wait_ge(S("G_free"), j * 2 + (before + c + 1))
                    n = j * 16 + 8 * c
                    v.tensor_tensor(hot2[:, c], iota[:, hf * HK:(hf + 1) * HK].unsqueeze(1).broadcast_to((P, 8, HK)),
                                    wide(R3[:, 1, ds(n, 8)], HK), ALU.is_equal).then_inc(S("hot2"), 1)
                    v.tensor_tensor(hot1[:, c], iota[:].unsqueeze(1).broadcast_to((P, 8, P)),
                                    wide(R3[:, 0, ds(n, 8)], P), ALU.is_equal).then_inc(S("hot1"), 1)
                rows(0, 0)
                rows(0, 1)
                with v.Fori(0, T // 16 - 1) as j:
                    for c in range(2):
                        product(j, c, c)
                        rows(j + 1, c)
                for c in range(2):
                    product(T // 16 - 1, c, c)

            @block.gpsimd
            def _(g):
                with g.Fori(0, T // 16) as j:
                    for c in range(2):
                        g.wait_ge(S("hot2"), j * 2 + (before + c + 1))
                        g.tensor_tensor(hot2[:, c], hot2[:, c], R3[:, 2, ds(j * 16 + 8 * c, 8)].unsqueeze(2)
                                        .broadcast_to((P, 8, HK)), ALU.mult).then_inc(S("gate2"), 1)

            @block.tensor
            def _(t):
                if hf == 0:
                    t.nop().then_inc(S("G_free"), 2)
                with t.Fori(0, T // 16) as j:
                    for c in range(2):
                        t.wait_ge(S("G_read"), j * 2 + (before + c + 1))
                        t.wait_ge(S("hot1"), j * 2 + (before + c + 1))
                        t.wait_ge(S("gate2"), j * 2 + (before + c + 1))
                        for q in range(8):
                            m = nc.tensor.matmul(PS[:, c, q * HK:(q + 1) * HK], hot1[:, c, q, :], hot2[:, c, q, :],
                                                 start=True, stop=True)
                        m.then_inc(S("G_free"), 1)

        done = hf * HK

        with nc.Block() as block:
            @block.sync
            def _(sp):
                if hf == 0:
                    sp.dma_start(x[:], x_saved).then_inc(S("x_again"), 16)
                stream(sp, halves[1])

            @block.tensor
            def _(t):
                def group(g, first, last):
                    for s in range(SLOTS):
                        t.wait_ge(S(f"lo{s}"), g + (V + 1))
                        t.wait_ge(S("g_lo"), g * 4 + (done + s + 1))
                        for tt in range(NT):
                            for c in range(4):
                                for p, (ga, wa) in enumerate(((hi_g, hi_w), (hi_g, lo_w), (lo_g, hi_w))):
                                    m = nc.tensor.matmul(PS[:, 4 * tt + c, :], ga[:, s, tt * P:(tt + 1) * P],
                                                         wa[s][:, c * 512:(c + 1) * 512],
                                                         start=first and s == 0 and p == 0,
                                                         stop=last and s == SLOTS - 1 and p == 2)
                        m.then_inc(S("unit_used"), 1)
                group(0, True, False)
                with t.Fori(1, NG - 1) as g:
                    group(g, False, False)
                group(NG - 1, False, True)

            @block.scalar
            def _(a):
                def high(g, s):
                    a.wait_ge(S("unit_used"), g * 4 + (4 * V + s - 3))
                    a.copy(hi_g[:, s, :], gg(g * 4 + s)).then_inc(S("g_hi"), 1)
                units(a, split_hi, V, high, 2)

            @block.vector
            def _(v):
                def low(g, s):
                    v.wait_ge(S("g_hi"), g * 4 + (done + s + 1))
                    v.tensor_tensor(lo_g[:, s, :], gg(g * 4 + s), hi_g[:, s, :].bitcast(F32), ALU.subtract)\
                        .then_inc(S("g_lo"), 1)
                units(v, split_lo, V, low, 2)
                v.wait_ge(S("x_again"), 16)
                v.wait_ge(S("unit_used"), 4 * (V + NG))
                for tt in range(NT):
                    v.tensor_tensor(x[:, tt, :], x[:, tt, :], PS[:, 4 * tt:4 * tt + 4, :].rearrange("p b c -> p (b c)"), ALU.add)

    peer_half(0)
    peer_half(1)

    bump[0] = base
    junkf = sb("junkf", (P, D))
    fgain = sb("fgain", (P, D))
    with nc.Block() as block:
        @block.scalar
        def _(a):
            a.dma_start(fgain[:], bcast("norm_final_g")).then_inc(S("fgain"), 16)
            for tt in range(NT):
                a.activation(junkf[:], x[:, tt, :], ACT.Square, accum_out=rstat[:, tt:tt + 1])
                a.drain()
                a.activation(rstat[:, 2 + tt:3 + tt], rstat[:, tt:tt + 1], ACT.Sqrt, bias=EPS, scale=1.0 / D)\
                    .then_inc(S("fn_sq"), 1)

        @block.vector
        def _(v):
            v.wait_ge(S("fgain"), 16)
            for tt in range(NT):
                v.wait_ge(S("fn_sq"), tt + 1)
                v.reciprocal(rstat[:, 4 + tt:5 + tt], rstat[:, 2 + tt:3 + tt])
                v.drain()
                v.scalar_tensor_tensor(out=x[:, tt, :], in0=x[:, tt, :], scalar=rstat[:, 4 + tt:5 + tt], in1=fgain[:],
                                       op0=ALU.mult, op1=ALU.mult)

    recycle()

    def gate_sigmoid(a, gate, sig, tt, tag):
        if tt:
            a.wait_ge(S(tag + "_gated"), 4 * tt)
        a.activation(sig[:], gate[:, tt], ACT.Sigmoid).then_inc(S(tag + "_sig"), 1)

    def gate_piece(g, k, gate, sig, wt, tag):
        tt, cs = k // 4, slice(k % 4 * 512, k % 4 * 512 + 512)
        g.wait_ge(S(tag + "_sig"), tt + 1)
        g.tensor_tensor(gate[:, tt, cs], gate[:, tt, cs], sig[:, cs], ALU.mult)
        g.drain()
        g.tensor_tensor(gate[:, tt, cs], gate[:, tt, cs], wt[:, cs], ALU.mult).then_inc(S(tag + "_gated"), 1)

    def std_of_sums(a, stt, tag):
        a.drain()
        a.activation(stt[:, 1], stt[:, 0], ACT.Sqrt, bias=EPS, scale=1.0 / P).then_inc(S(tag + "_std"), 1)

    def finish_heads(v, o, gate, stt, tag):
        v.wait_ge(S(tag + "_std"), 1)
        v.reciprocal(stt[:, 2], stt[:, 1])
        v.drain()
        v.wait_ge(S(tag + "_gated"), 4 * NT)
        for tt in range(NT):
            for h in range(HH):
                hs_ = slice(h * P, (h + 1) * P)
                v.scalar_tensor_tensor(out=o[:, tt, hs_], in0=o[:, tt, hs_], scalar=stt[:, 2, tt * HH + h:tt * HH + h + 1],
                                       in1=gate[:, tt, hs_], op0=ALU.mult, op1=ALU.mult)

    def scale_heads(v, o, sq, stt, tag):
        cols = lambda ap, m: ap[:, :, ds(m * 512, 512)]
        st_ = lambda i, m: stt[:, i].rearrange("p (t h) -> p t h", t=NT)[:, :, ds(m * 4, 4)]
        heads = lambda ap: ap.rearrange("p t (h c) -> p t h c", c=P)

        def sums(m):
            v.drain()
            v.tensor_tensor(sq[:], cols(o, m), cols(o, m), ALU.mult)
            v.drain()
            v.tensor_reduce(st_(0, m), heads(sq[:]), X, ALU.add).then_inc(S(tag + "_ss"), 1)

        def scaled(m):
            v.wait_ge(S(tag + "_std"), m + 1)
            v.reciprocal(st_(2, m), st_(1, m))
            v.drain()
            v.tensor_tensor(heads(cols(o, m)), heads(cols(o, m)), st_(2, m).unsqueeze(3).broadcast_to((P, NT, 4, P)), ALU.mult)
        return dict(before=sums, ending=scaled)

    def head_std(a, stt, tag):
        st_ = lambda i, m: stt[:, i].rearrange("p (t h) -> p t h", t=NT)[:, :, ds(m * 4, 4)]

        def std(m):
            a.wait_ge(S(tag + "_ss"), m + 1)
            a.activation(st_(1, m), st_(0, m), ACT.Sqrt, bias=EPS, scale=1.0 / P).then_inc(S(tag + "_std"), 1)
        return dict(before=std)

    norm_T("a_norm_w")
    fz = sb("fz", (P, NT, D))
    hq = sb("hq", (P, NT, D))
    hv = sb("hv", (P, NT, D))
    hg = sb("hg", (P, NT, D))
    hk = sb("hk", (P, NT, D))
    lbt = sb("lbt", (P, D))
    after_h = bump[0]
    lu = sb("lu", (P, 512))
    lt = sb("lt", (P, 512))
    lbs = hv[:, 0, :]
    with nc.Block() as block:
        @block.sync
        def _(sp):
            sp.dma_start(lbt[:], bcast("a_lb_logits_2")).then_inc(S("lb_in"), 16)
            stream(sp, "a_in")

        @block.tensor
        def _(t):
            dense(t, "a_in", 16, 16, X_)

        @block.vector
        def _(v):
            v.wait_ge(S("lb_in"), 16)
            v.tensor_tensor(lbs, lbt[:], lbt[:], ALU.subtract)
            v.drain().then_inc(S("lb_d"), 1)
            v.wait_ge(S("lb_e"), 1)
            v.reciprocal(lbt[:], lbs)
            v.drain()
            v.tensor_tensor(lbt[:], lbt[:], lbs, ALU.mult)
            v.drain()
            v.tensor_tensor(lbt[:], lbt[:], lbt[:], ALU.subtract)
            v.drain()

            def forget(tt):
                at_ = lambda c: (fz[:, tt, ds(c * 512, 512)], lbt[:, ds(c * 512, 512)], hk[:, tt, ds(c * 512, 512)])

                def clamp(c):
                    f, l, k = at_(c)
                    if tt:
                        v.wait_ge(S("fz_in"), 1)
                    v.tensor_scalar(lu[:], f, -80.0, None, ALU.max).then_inc(S("f_clamp"), 1)

                def finish(c):
                    f, l, k = at_(c)
                    v.wait_ge(S("f_u"), c + (4 * tt + 1))
                    v.tensor_tensor(lu[:], lu[:], l, ALU.mult).then_inc(S("f_lbu"), 1)
                    v.tensor_scalar(f, f, 80.0, 0.0, ALU.add, ALU.min)
                    v.drain()
                    v.tensor_tensor(f, f, lt[:], ALU.subtract)
                    v.drain()
                    v.scalar_tensor_tensor(out=lt[:], in0=l, scalar=-1.0, in1=k, op0=ALU.mult, op1=ALU.mult)
                    v.drain()
                    v.tensor_tensor(k, k, lt[:], ALU.add)
                    v.wait_ge(S("f_ln"), c + (4 * tt + 1))
                    v.tensor_tensor(f, f, lu[:], ALU.add)
                    v.drain()
                return dict(before=clamp, ending=finish)
            evac(v, split_lo, "a_in", 4, 16, [0], to(fz)(v, False), last=False)
            v.drain()
            evac(v, split_lo, "a_in", 4, 16, [0], to(hq)(v, False), at=4, first=False, last=False, **forget(0))
            evac(v, split_lo, "a_in", 4, 16, [0], to(hv)(v, False), at=8, first=False, last=False, **forget(1))
            evac(v, split_lo, "a_in", 4, 16, [0], to(hg)(v, False), at=12, first=False)

        @block.scalar
        def _(a):
            a.wait_ge(S("lb_d"), 1)
            a.activation(lbs, lbs, ACT.Exp).then_inc(S("lb_e"), 1)

            def forget_functions(tt):
                def first_(j, par):
                    k = hk[:, tt, ds(j * 1024 + par * 512, 512)]
                    a.wait_ge(S("f_clamp"), j * 2 + (4 * tt + par + 1))
                    a.activation(k, fz[:, tt, ds(j * 1024 + par * 512, 512)], ACT.Sigmoid, scale=-1.0)
                    a.activation(lu[:], lu[:], ACT.Exp, scale=-1.0)
                    a.drain()
                    a.activation(lt[:], lu[:], ACT.Ln, bias=1.0)
                    a.drain().then_inc(S("f_u"), 1)

                def second(c):
                    a.wait_ge(S("f_lbu"), c + (4 * tt + 1))
                    a.activation(lu[:], lu[:], ACT.Ln, bias=1.0).then_inc(S("f_ln"), 1)
                return dict(after=first_, ending=second)
            evac(a, split_hi, "a_in", 4, 16, [1], to(fz)(a, True), last=False)
            a.drain().then_inc(S("fz_in"), 1)
            evac(a, split_hi, "a_in", 4, 16, [1], to(hq)(a, True), at=4, first=False, last=False, **forget_functions(0))
            evac(a, split_hi, "a_in", 4, 16, [1], to(hv)(a, True), at=8, first=False, last=False, **forget_functions(1))
            evac(a, split_hi, "a_in", 4, 16, [1], to(hg)(a, True), at=12, first=False)
    chunks[0] += 16

    bump[0] = after_h
    LV = LEV + 1
    HN = HH * NT
    dm = sb("dm", (P, LEV + 2, P))
    lmask = sb("lmask", (P, LV, P))
    EE = sb("EE", (P, 2, LV, P))
    AS = sb("AS", (P, 2, P))
    sig = sb("sig", (P, D))
    osq = sb("osq", (P, 4, P))
    Eq = [over(f"Eq{i}", (P, LV, P), F32, spare_at + i * LV * P * 4) for i in range(2)]
    Ek = [over(f"Ek{i}", (P, LV, P), F32, spare_at + (2 + i) * LV * P * 4) for i in range(2)]
    Ek += [sb(f"Ek{2 + i}", (P, LV, P)) for i in range(2)]
    qkT = sb("qkT", (P, 2, 2, P))
    AM = xT[:].rearrange("p k c -> p (k c)")[:, 0:1024].rearrange("p (l c) -> p l c", l=LV)
    AX = xT[:].rearrange("p k c -> p (k c)")[:, 1024:1152]
    hw = xT[:].rearrange("p k c -> p (k c)")[:, 2048:4096]
    hst = xT[:].rearrange("p k c -> p (k c)")[:, 1152:1152 + 128].rearrange("p (a b) -> p a b", a=4)
    with nc.Block() as block:
        @block.sync
        def _(sp):
            sp.dma_start(dm[:].rearrange("p l c -> p (l c)"), consts["dm"]).then_inc(S("lev_in"), 16)
            sp.dma_start(lmask[:].rearrange("p l c -> p (l c)"), consts["levels"]).then_inc(S("lev_in"), 16)
            sp.dma_start(hw, bcast("a_out_norm_w_2")).then_inc(S("lev_in"), 16)

        @block.tensor
        def _(t):
            t.wait_ge(S("lev_in"), 48)

            def decays(n):
                h, tt = divmod(n, 2)
                hs_ = slice(h * P, (h + 1) * P)
                if n:
                    t.wait_ge(S("h_exp"), n)
                    t.wait_ge(S("h_qk"), n)
                for b in range(2):
                    nc.tensor.matmul(PS[:, b, :], fz[:, tt, hs_], dm[:, tt + 4 * b:tt + 4 * b + 4, :].rearrange("p l c -> p (l c)"),
                                     start=True, stop=True)
                nc.tensor.transpose(PS[:, 2, 0:P], hq[:, tt, hs_], ident[:])
                nc.tensor.transpose(PS[:, 2, P:2 * P], hk[:, tt, hs_], ident[:]).then_inc(S("h_D"), 1)

            def weights(n):
                h, tt = divmod(n, 2)
                t.wait_ge(S("h_Eq"), n + 1)
                t.wait_ge(S("h_Ek"), n + 1)
                if n:
                    t.wait_ge(S("h_AM"), n)
                if tt and h:
                    t.wait_ge(S("h_AX"), h)
                lev = range(1, LV) if tt == 0 else range(0, LEV)
                for k, l in enumerate(lev):
                    nc.tensor.matmul(PS[:, 3 + k // 4, (k % 4) * P:(k % 4 + 1) * P], Ek[n % 4][:, l, :], Eq[n % 2][:, l, :],
                                     start=True, stop=True)
                m = nc.tensor.matmul(PS[:, 4, 3 * P:4 * P], qkT[:, n % 2, 1, :], qkT[:, n % 2, 0, :], start=True, stop=True)
                if tt:
                    m = nc.tensor.matmul(PS[:, 5, 0:P], Ek[(n - 1) % 4][:, 0, :], Eq[n % 2][:, LV - 1, :], start=True, stop=True)
                m.then_inc(S("h_A"), 1)

            def values(n):
                h, tt = divmod(n, 2)
                hs_ = slice(h * P, (h + 1) * P)
                t.wait_ge(S("h_AS"), n + 1)
                if n >= 2:
                    t.wait_ge(S("h_out"), n - 1)
                m = nc.tensor.matmul(PS[:, 6 + n % 2, 0:P], AS[:, n % 2, :], hv[:, tt, hs_], start=True, stop=tt == 0)
                if tt:
                    t.wait_ge(S("h_AX"), h + 1)
                    m = nc.tensor.matmul(PS[:, 6 + n % 2, 0:P], AX, hv[:, 0, hs_], start=False, stop=True)
                m.then_inc(S("h_pv"), 1)

            decays(0)
            for n in range(HN):
                if n + 1 < HN:
                    decays(n + 1)
                weights(n)
                if n:
                    values(n - 1)
            values(HN - 1)

        @block.scalar
        def _(a):
            def cross(n):
                if n % 2:
                    a.wait_ge(S("h_A"), n + 1)
                    if n >= 2:
                        a.wait_ge(S("h_pv"), n - 1)
                    a.copy(AX, PS[:, 5, 0:P]).then_inc(S("h_AX"), 1)

            def out(n):
                h, tt = divmod(n, 2)
                a.wait_ge(S("h_pv"), n + 1)
                a.copy(hq[:, tt, h * P:(h + 1) * P], PS[:, 6 + n % 2, 0:P])
                a.activation(osq[:, n % 4], PS[:, 6 + n % 2, 0:P], ACT.Square, accum_out=hst[:, 0, tt * HH + h:tt * HH + h + 1])\
                    .then_inc(S("h_out"), 1)

            gate_sigmoid(a, hg, sig, 0, "h")
            for n in range(HN + 2):
                if n == HN // 2:
                    gate_sigmoid(a, hg, sig, 1, "h")
                if n < HN:
                    a.wait_ge(S("h_D"), n + 1)
                    if n >= 2:
                        a.wait_ge(S("h_A"), n - 1)
                    a.copy(qkT[:, n % 2], PS[:, 2, 0:2 * P].rearrange("p (a c) -> p a c", a=2)).then_inc(S("h_qk"), 1)
                    a.activation(EE[:, n % 2], PS[:, 0:2, :].rearrange("p b (l c) -> p (b l) c", l=4), ACT.Exp)\
                        .then_inc(S("h_exp"), 1)
                if 1 <= n <= HN:
                    cross(n - 1)
                if n >= 2:
                    out(n - 2)
            std_of_sums(a, hst, "h")

        @block.gpsimd
        def _(g):
            for n in range(HN):
                g.wait_ge(S("h_exp"), n + 1)
                g.wait_ge(S("h_qk"), n + 1)
                if n >= 4:
                    g.wait_ge(S("h_A"), n - 2)
                if n == 0:
                    g.wait_ge(S("lev_in"), 48)
                g.tensor_tensor(Ek[n % 4][:], EE[:, n % 2], qkT[:, n % 2, 1, :].unsqueeze(1).broadcast_to((P, LV, P)), ALU.mult)\
                    .then_inc(S("h_Ek"), 1)
                if n % 4 == 2:
                    gate_piece(g, n // 4, hg, sig, hw, "h")

        @block.vector
        def _(v):
            v.wait_ge(S("lev_in"), 48)
            for n in range(HN + 1):
                if n < HN:
                    v.wait_ge(S("h_exp"), n + 1)
                    v.wait_ge(S("h_qk"), n + 1)
                    if n >= 2:
                        v.wait_ge(S("h_A"), n - 1)
                    v.tensor_tensor(Eq[n % 2][:], EE[:, n % 2], qkT[:, n % 2, 0, :].unsqueeze(1).broadcast_to((P, LV, P)), ALU.mult)\
                        .then_inc(S("h_Eq"), 1)
                if n:
                    v.wait_ge(S("h_A"), n)
                    v.drain()
                    v.tensor_tensor(AM, PS[:, 3:5, :].rearrange("p b (l c) -> p (b l) c", l=4), lmask[:], ALU.mult)\
                        .then_inc(S("h_AM"), 1)
                    v.drain()
                    if n >= 3:
                        v.wait_ge(S("h_pv"), n - 2)
                    v.tensor_reduce(AS[:, (n - 1) % 2, :], AM.rearrange("p l c -> p c l"), X, ALU.add).then_inc(S("h_AS"), 1)
            v.wait_ge(S("h_out"), HN)
            finish_heads(v, hq, hg, hst, "h")
    turn(hq)
    project_residual("a_out")

    norm_T("kv_norm_w")
    fk = sb("fk", (P, NT, D))
    fv = sb("fv", (P, NT, D))
    fq = sb("fq", (P, NT, D))
    fg = sb("fg", (P, NT, D))
    fst = sb("fst", (P, 4, NT * HH))
    FT_ = sb("FT_", (HH, T))
    fxend = bump[0]
    ftmp = sb("ftmp", (P, NT, D))
    fsq = sb("fsq", (P, NT, 512))
    wf = sb("wf", (P, KC, HH))
    fb = sb("fb", (P, HH))
    tri = sb("tri", (P, P))
    one = sb("one", (P, P))
    lf = sb("lf", (P, 4, NT, HH))
    hi_f = over("hi_f", (P, KC, HH), F32R, bump[0])
    bump[0] += KC * HH * 4
    lo_f = over("lo_f", (P, KC, HH), F32R, bump[0])
    bump[0] += KC * HH * 4
    with nc.Block() as block:
        @block.sync
        def _(sp):
            for d_, s_ in ((wf[:], dram["f_w"]), (fb[:], bcast("kv_f_bias_2")), (tri[:], consts["tri"]), (one[:], consts["ones"])):
                sp.dma_start(d_, s_).then_inc(S("fx_in"), 16)
            stream(sp, "kv")

        @block.tensor
        def _(t):
            t.wait_ge(S("fx_in"), 64)
            t.wait_ge(S("wf_split"), 1)
            for tt in range(NT):
                for k in range(KC):
                    for p, (xa, fa) in enumerate(((hi_x, hi_f), (hi_x, lo_f), (lo_x, hi_f))):
                        m = nc.tensor.matmul(PS[:, 4 + tt, 0:HH], xa[:, k, tt * P:(tt + 1) * P], fa[:, k, :],
                                             start=(k == 0 and p == 0), stop=(k == KC - 1 and p == 2))
            m.then_inc(S("fz_ps"), 1)
            t.wait_ge(S("lf"), 1)
            nc.tensor.matmul(PS[0:HH, 6, 0:P], lf[:, 3, 0, :], tri[:], start=True, stop=True)
            nc.tensor.matmul(PS[0:HH, 6, P:2 * P], lf[:, 3, 0, :], one[:], start=True, stop=False)
            nc.tensor.matmul(PS[0:HH, 6, P:2 * P], lf[:, 3, 1, :], tri[:], start=False, stop=True).then_inc(S("F_T"), 1)
            dense(t, "kv", 8, 16, X_)

        @block.vector
        def _(v):
            v.wait_ge(S("fx_in"), 64)
            v.tensor_copy(hi_f[:], wf[:])
            v.drain()
            v.tensor_tensor(lo_f[:], wf[:], hi_f[:].bitcast(F32), ALU.subtract).then_inc(S("wf_split"), 1)
            begin(v, split_lo, "kv", 16)
            v.wait_ge(S("fz_ps"), 1)
            for tt in range(NT):
                v.tensor_tensor(lf[:, 0, tt, :], PS[:, 4 + tt, 0:HH], fb[:], ALU.add)
            v.drain()
            v.tensor_scalar(lf[:, 1], lf[:, 0], -1.0, 0.0, ALU.mult, ALU.max)
            v.tensor_scalar(lf[:, 2], lf[:, 0], -1.0, None, ALU.mult)
            v.drain()
            v.tensor_tensor(lf[:, 2], lf[:, 0], lf[:, 2], ALU.max)
            v.drain().then_inc(S("f_abs"), 1)
            v.wait_ge(S("f_log"), 1)
            v.tensor_tensor(lf[:, 3], lf[:, 1], lf[:, 2], ALU.add)
            v.drain().then_inc(S("lf"), 1)
            evac(v, split_lo, "kv", 4, 16, [0], to(fk)(v, False), first=False, last=False)
            v.wait_ge(S("fk_in"), 1)
            evac(v, split_lo, "kv", 4, 16, [0], to(fv)(v, False), at=4, first=False, **scale_heads(v, fk, fsq, fst, "fk"))

        @block.scalar
        def _(a):
            begin(a, split_hi, "kv", 16)
            a.wait_ge(S("f_abs"), 1)
            a.activation(lf[:, 2], lf[:, 2], ACT.Exp, scale=-1.0)
            a.drain()
            a.activation(lf[:, 2], lf[:, 2], ACT.Ln, bias=1.0).then_inc(S("f_log"), 1)
            a.wait_ge(S("F_T"), 1)
            a.copy(FT_[:], PS[0:HH, 6, 0:T])
            evac(a, split_hi, "kv", 4, 16, [1], to(fk)(a, True), first=False, last=False)
            a.drain().then_inc(S("fk_in"), 1)
            evac(a, split_hi, "kv", 4, 16, [1], to(fv)(a, True), at=4, first=False, **head_std(a, fst, "fk"))
    chunks[0] += 8

    norm_T("b_norm_w", stats=False, xs=ftmp)
    with nc.Block() as block:
        @block.sync
        def _(sp):
            stream(sp, "b_in")

        @block.tensor
        def _(t):
            dense(t, "b_in", 8, 16, X_)

        @block.vector
        def _(v):
            evac(v, split_lo, "b_in", 4, 16, [0], to(fq)(v, False), last=False)
            v.wait_ge(S("fq_in"), 1)
            evac(v, split_lo, "b_in", 4, 16, [0], to(fg)(v, False), at=4, first=False, **scale_heads(v, fq, fsq, fst, "fq"))

        @block.scalar
        def _(a):
            evac(a, split_hi, "b_in", 4, 16, [1], to(fq)(a, True), last=False)
            a.drain().then_inc(S("fq_in"), 1)
            evac(a, split_hi, "b_in", 4, 16, [1], to(fg)(a, True), at=4, first=False, **head_std(a, fst, "fq"))
    chunks[0] += 8

    bump[0] = fxend
    fqT = sb("fqT", (P, 2, T))
    fkT = sb("fkT", (P, 2, T))
    gq = sb("gq", (P, 2))
    fsig = sb("fsig", (P, D))
    fosq = sb("fosq", (P, 4, P))
    sel = xT[0:HH, 0:8, :].rearrange("p k c -> p (k c)").rearrange("p (h c) -> p h c", h=HH)
    fw = xT[:].rearrange("p k c -> p (k c)")[:, 2048:4096]
    causal = sb("causal", (P, P))
    fp = sb("fp", (P, 2, T))
    fpT = sb("fpT", (P, 2, 2, P))
    fs = sb("fs", (P, 4, 2 * HH))
    with nc.Block() as block:
        @block.sync
        def _(sp):
            for d_, s_ in ((gq[:, 0:1], dram["q_norm"]), (gq[:, 1:2], dram["k_norm"]), (causal[:], consts["causal"]),
                           (sel.rearrange("p h c -> p (h c)"), consts["sel"][0:HH]), (fw, bcast("b_out_norm_w_2"))):
                sp.dma_start(d_, s_).then_inc(S("fa_in"), 16)

        @block.tensor
        def _(t):
            t.wait_ge(S("fa_in"), 80)

            def turn_head(h):
                if h:
                    t.wait_ge(S("fa_T"), h)
                for k, src in enumerate((fq, fk)):
                    for tt in range(NT):
                        m = nc.tensor.transpose(PS[:, k, tt * P:(tt + 1) * P], src[:, tt, h * P:(h + 1) * P], ident[:])
                m.then_inc(S("fa_turn"), 1)

            def scores(n):
                h, tt = divmod(n, 2)
                w = P * (tt + 1)
                if tt == 0:
                    t.wait_ge(S("fa_T"), h + 1)
                if n >= 2:
                    t.wait_ge(S("fa_s"), n - 1)
                nc.tensor.matmul(PS[:, 2 + n % 2, 0:w], fqT[:, h % 2, tt * P:(tt + 1) * P], fkT[:, h % 2, 0:w], start=True, stop=False)
                nc.tensor.matmul(PS[:, 2 + n % 2, 0:w], sel[:, h, :], FT_[:, 0:w], start=False, stop=True).then_inc(S("fa_qk"), 1)

            turn_head(0)
            turn_head(1)
            scores(0)
            for n in range(2 * HH):
                h, tt = divmod(n, 2)
                if n + 1 < 2 * HH:
                    scores(n + 1)
                if tt == 1 and h + 2 < HH:
                    turn_head(h + 2)
                t.wait_ge(S("fa_p"), n + 1)
                if n >= 2:
                    t.wait_ge(S("fa_pT"), n - 1)
                for k in range(tt + 1):
                    m = nc.tensor.transpose(PS[:, 4 + n % 2, k * P:(k + 1) * P], fp[:, n % 2, k * P:(k + 1) * P], ident[:])
                m.then_inc(S("fa_pTps"), 1)
                t.wait_ge(S("fa_pT"), n + 1)
                if n >= 2:
                    t.wait_ge(S("fa_o"), n - 1)
                for k in range(tt + 1):
                    m = nc.tensor.matmul(PS[:, 6 + n % 2, 0:P], fpT[:, n % 2, k, :], fv[:, k, h * P:(h + 1) * P], start=(k == 0), stop=(k == tt))
                m.then_inc(S("fa_pv"), 1)

        @block.vector
        def _(v):
            v.wait_ge(S("fa_in"), 80)

            def evac_T(h):
                v.wait_ge(S("fa_turn"), h + 1)
                if h >= 2:
                    v.wait_ge(S("fa_qk"), 2 * h - 2)
                v.tensor_scalar(fqT[:, h % 2], PS[:, 0, 0:T], gq[:, 0:1], FSCALE, ALU.mult, ALU.mult)
                v.tensor_scalar(fkT[:, h % 2], PS[:, 1, 0:T], gq[:, 1:2], None, ALU.mult)
                v.drain().then_inc(S("fa_T"), 1)
            evac_T(0)
            evac_T(1)
            for n in range(2 * HH):
                h, tt = divmod(n, 2)
                w = P * (tt + 1)
                v.wait_ge(S("fa_qk"), n + 1)
                if n >= 2:
                    v.wait_ge(S("fa_pTps"), n - 1)
                v.tensor_tensor(fp[:, n % 2, w - P:w], PS[:, 2 + n % 2, w - P:w], causal[:], ALU.add)
                if tt:
                    v.tensor_copy(fp[:, n % 2, 0:P], PS[:, 2 + n % 2, 0:P])
                v.drain().then_inc(S("fa_s"), 1)
                v.tensor_reduce(fs[:, 0, n:n + 1], fp[:, n % 2, 0:w], X, ALU.max)
                v.drain()
                v.tensor_scalar(fs[:, 1, n:n + 1], fs[:, 0, n:n + 1], -1.0, None, ALU.mult).then_inc(S("fa_max"), 1)
                if tt == 1 and h + 2 < HH:
                    evac_T(h + 2)
                v.wait_ge(S("fa_exp"), n + 1)
                v.reciprocal(fs[:, 3, n:n + 1], fs[:, 2, n:n + 1])
                v.drain()
                v.tensor_scalar(fp[:, n % 2, 0:w], fp[:, n % 2, 0:w], fs[:, 3, n:n + 1], None, ALU.mult).then_inc(S("fa_p"), 1)
            v.wait_ge(S("fa_o"), 2 * HH)
            finish_heads(v, fq, fg, fst, "f")

        @block.scalar
        def _(a):
            def out(n):
                h, tt = divmod(n, 2)
                a.wait_ge(S("fa_pv"), n + 1)
                a.wait_ge(S("fa_turn"), h + 1)
                a.copy(fq[:, tt, h * P:(h + 1) * P], PS[:, 6 + n % 2, 0:P])
                a.activation(fosq[:, n % 4], PS[:, 6 + n % 2, 0:P], ACT.Square, accum_out=fst[:, 0, tt * HH + h:tt * HH + h + 1])\
                    .then_inc(S("fa_o"), 1)
            gate_sigmoid(a, fg, fsig, 0, "f")
            for n in range(2 * HH):
                w = P * (n % 2 + 1)
                if n == HH:
                    gate_sigmoid(a, fg, fsig, 1, "f")
                a.wait_ge(S("fa_max"), n + 1)
                a.activation(fp[:, n % 2, 0:w], fp[:, n % 2, 0:w], ACT.Exp, bias=fs[:, 1, n:n + 1], accum_out=fs[:, 2, n:n + 1])\
                    .then_inc(S("fa_exp"), 1)
                a.wait_ge(S("fa_pTps"), n + 1)
                if n >= 2:
                    a.wait_ge(S("fa_pv"), n - 1)
                a.copy(fpT[:, n % 2, 0:n % 2 + 1, :], PS[:, 4 + n % 2, 0:w].rearrange("p (k c) -> p k c", c=P)).then_inc(S("fa_pT"), 1)
                if n:
                    out(n - 1)
            out(2 * HH - 1)
            std_of_sums(a, fst, "f")

        @block.gpsimd
        def _(g):
            g.wait_ge(S("fa_in"), 80)
            for k in range(4 * NT):
                gate_piece(g, k, fg, fsig, fw, "f")
    turn(fq)
    project_residual("b_out")
    with nc.Block() as block:
        @block.sync
        def _(sp):
            sp.dma_start(dram["out"].rearrange("(t p) d -> p t d", p=P), x[:]).then_inc(S("x_back"), 16)
            sp.wait_ge(S("x_back"), 32)


def dense_units(w):
    k, n = w.shape
    c = -(-n // 512)
    w = np.pad(w, ((0, 0), (0, c * 512 - n)))
    return w.reshape(k // 512, 4, P, c, 512).transpose(3, 0, 2, 1, 4).reshape(-1, P, UNIT)


def layout(inputs):
    a = {k: np.asarray(v) for k, v in inputs.items()}
    w = a["w_in"][0]
    o = np.cumsum([0, RW, RW, RW, 288, 1024, 256, 512, 64, 8, 4096])
    r, k, v, zs, q, ckv, iq, ik, iw, gt = (w[:, o[i]:o[i + 1]] for i in range(10))
    w_in = [r, k, v, zs, q, iq, np.concatenate([ckv, iw, ik], 1), gt]
    u = a["peer_u"][0].reshape(PK, PK, KC, P).transpose(1, 3, 2, 0).reshape(PK, P, UNIT)
    vv = a["peer_v"][0].reshape(PK, PK, D).transpose(1, 0, 2)
    kv = a["kv_w_2"]
    parts = [*(dense_units(m) for m in w_in), dense_units(a["w_branch_rwkv"][0]), dense_units(a["w_branch_dsa"][0]),
             dense_units(a["w_out"][0]), dense_units(a["w_peer_query"][0]), u[:PK // 2], vv[:PK // 2], u[PK // 2:], vv[PK // 2:]]
    az = a["a_w_in_2"][0]
    parts += [dense_units(az[:, i * D:(i + 1) * D]) for i in (1, 0, 2, 3)]
    parts += [dense_units(a["a_w_out_2"][0]), dense_units(kv[:, :2 * D]), dense_units(a["b_w_in_2"][0]),
              dense_units(a["b_w_out_2"][0])]
    d = {"wstream": np.concatenate(parts)}
    assert len(d["wstream"]) == GROUPS * SLOTS
    d["x"] = a["x"][0]
    col = lambda g: np.ascontiguousarray(g.reshape(KC, P).T)
    for n, g in (("norm_mix_g", a["norm_mix_g"]), ("norm_ffn_g", a["norm_ffn_g"]), ("a_norm_w", a["a_norm_w_2"]),
                 ("kv_norm_w", a["kv_norm_w_2"]), ("b_norm_w", a["b_norm_w_2"])):
        d[n] = col(g.reshape(-1))
    for n in ("shift_mix", "w0", "a0", "k_k", "k_a", "r_k", "ln_x_w", "ln_x_b", "kv_norm_g", "norm_final_g",
              "a_lb_logits_2", "a_out_norm_w_2", "b_out_norm_w_2", "kv_f_bias_2"):
        d[n] = a[n].reshape(-1)
    d["k_norm"] = a["k_norm_w_2"].reshape(P, 1)
    d["q_norm"] = a["b_q_norm_w_2"].reshape(P, 1)
    d["up"] = np.concatenate([a["w_decay_up"][0], a["w_icl_up"][0]], 0)
    d["gate_up"] = a["w_gate_up"][0]
    for n in ("w_uk", "w_uv"):
        d[n] = a[n][0].transpose(1, 0, 2).reshape(2, P, RW).transpose(1, 0, 2)
    d["rel_bias"] = a["rel_bias"]
    d["sub_keys"] = a["peer_sub_keys"][0].transpose(3, 0, 1, 2)
    d["f_w"] = kv[:, 2 * D:].reshape(KC, P, HH).transpose(1, 0, 2)
    return {k: np.ascontiguousarray(v) for k, v in d.items()}


def kernel(**inputs):
    import concourse.bacc as _bacc
    from concourse import mybir as _mybir
    from concourse.bass_utils import run_bass_kernel_spmd as _run

    arrays = {"in_" + k: v for k, v in layout(inputs).items()}
    fixed = {"c_" + k: v for k, v in constants().items()}
    arrays.update(fixed)
    nc = _bacc.Bacc("TRN2", target_bir_lowering=False, num_devices=1)
    aps = {k: nc.dram_tensor(k, v.shape, _mybir.dt.float32, kind="ExternalInput").ap() for k, v in arrays.items()}
    dram = {k[3:]: v for k, v in aps.items() if k.startswith("in_")}
    consts = {k[2:]: v for k, v in aps.items() if k.startswith("c_")}
    dram["out"] = nc.dram_tensor("out", (T, D), _mybir.dt.float32, kind="ExternalOutput").ap()
    build(nc, dram, consts)
    r = _run(nc, [arrays], core_ids=[0])
    return r.results[0]["out"].reshape(1, T, D)
```
